# Optimizing a Trainium2 kernel written in Bass

```python
import jax, jax.numpy as jnp
from jax import lax
import numpy as np

D_MODEL = 2048
BATCH = 1
SEQ = 256
DEPTH = 2

N_MIXERS = 2
N_HEADS = 16
HEAD_DIM = D_MODEL // N_HEADS
ATTN_WIDTH = N_HEADS * HEAD_DIM
MOBA_BLOCK = 256
MOBA_TOPK = 3
Q_CHUNK = 8
ROPE_THETA = 10000.0
CONV_WIDTH = D_MODEL
CONV_K = 31
RMS_EPS = 1e-6
LN_EPS = 1e-5
NEG = -1e30
N_ATTN_LAYERS = (DEPTH + 1) // 2
N_CONV_LAYERS = DEPTH // 2

kernel_name = "hybrid_moba_conformer_sandwich"

def rms_norm(x, g):
    xf = x.astype(jnp.float32)
    y = xf * lax.rsqrt(jnp.mean(xf * xf, axis=-1, keepdims=True) + RMS_EPS)
    return (y * g.astype(jnp.float32)).astype(x.dtype)

def layer_norm(x, g, b):
    xf = x.astype(jnp.float32)
    mu = jnp.mean(xf, axis=-1, keepdims=True)
    var = jnp.mean(jnp.square(xf - mu), axis=-1, keepdims=True)
    y = (xf - mu) * lax.rsqrt(var + LN_EPS)
    return (y * g.astype(jnp.float32) + b.astype(jnp.float32)).astype(x.dtype)

def apply_rope(t):
    s, d = t.shape[2], t.shape[3]
    half = d // 2
    inv_freq = 1.0 / (ROPE_THETA ** (jnp.arange(half, dtype=jnp.float32) * 2.0 / d))
    ang = jnp.arange(s, dtype=jnp.float32)[:, None] * inv_freq[None, :]
    cos, sin = jnp.cos(ang), jnp.sin(ang)
    tf = t.astype(jnp.float32)
    t1, t2 = tf[..., :half], tf[..., half:]
    return jnp.concatenate([t1 * cos - t2 * sin, t2 * cos + t1 * sin], axis=-1).astype(t.dtype)

def moba_attention(q, k, v):
    b, h, s, d = q.shape
    nb = -(-s // MOBA_BLOCK)
    pad = nb * MOBA_BLOCK - s
    kp = jnp.pad(k, ((0, 0), (0, 0), (0, pad), (0, 0)))
    vp = jnp.pad(v, ((0, 0), (0, 0), (0, pad), (0, 0)))
    k_blk = kp.reshape(b, h, nb, MOBA_BLOCK, d)
    v_blk = vp.reshape(b, h, nb, MOBA_BLOCK, d)
    k_mean = jnp.mean(k_blk.astype(jnp.float32), axis=3)
    scale = d ** -0.5

    q_blk = jnp.arange(s) // MOBA_BLOCK
    gate = jnp.einsum('bhsd,bhnd->bhsn', q.astype(jnp.float32), k_mean)
    past = jnp.arange(nb)[None, :] < q_blk[:, None]
    gate = jnp.where(past, gate, NEG)
    kk = min(MOBA_TOPK, nb)
    _, sel = lax.top_k(gate, kk)
    sel_valid = sel < q_blk[:, None]

    b_idx = jnp.arange(b)[:, None, None, None]
    h_idx = jnp.arange(h)[None, :, None, None]
    n_chunks = s // Q_CHUNK

    def chunk(c):
        start = c * Q_CHUNK
        qc = lax.dynamic_slice_in_dim(q, start, Q_CHUNK, axis=2)
        selc = lax.dynamic_slice_in_dim(sel, start, Q_CHUNK, axis=2)
        validc = lax.dynamic_slice_in_dim(sel_valid, start, Q_CHUNK, axis=2)
        j = start // MOBA_BLOCK
        k_own = lax.dynamic_index_in_dim(k_blk, j, axis=2, keepdims=False)
        v_own = lax.dynamic_index_in_dim(v_blk, j, axis=2, keepdims=False)
        k_sel = k_blk[b_idx, h_idx, selc]
        v_sel = v_blk[b_idx, h_idx, selc]
        s_own = jnp.einsum('bhqd,bhkd->bhqk', qc, k_own).astype(jnp.float32) * scale
        s_sel = jnp.einsum('bhqd,bhqnkd->bhqnk', qc, k_sel).astype(jnp.float32) * scale
        qpos = start + jnp.arange(Q_CHUNK)
        kpos = j * MOBA_BLOCK + jnp.arange(MOBA_BLOCK)
        s_own = jnp.where(kpos[None, :] <= qpos[:, None], s_own, NEG)
        s_sel = jnp.where(validc[..., None], s_sel, NEG)
        scores = jnp.concatenate(
            [s_own, s_sel.reshape(b, h, Q_CHUNK, kk * MOBA_BLOCK)], axis=-1)
        p = jax.nn.softmax(scores, axis=-1).astype(v.dtype)
        p_own = p[..., :MOBA_BLOCK]
        p_sel = p[..., MOBA_BLOCK:].reshape(b, h, Q_CHUNK, kk, MOBA_BLOCK)
        return (jnp.einsum('bhqk,bhkd->bhqd', p_own, v_own)
                + jnp.einsum('bhqnk,bhqnkd->bhqd', p_sel, v_sel))

    outs = lax.map(chunk, jnp.arange(n_chunks))
    return outs.transpose(1, 2, 0, 3, 4).reshape(b, h, s, d)

def moba_mixer(hn, w_in, w_out):
    b, s, _ = hn.shape
    proj = hn @ w_in
    q, k, v, z = jnp.split(proj, 4, axis=-1)
    to_heads = lambda t: t.reshape(b, s, N_HEADS, HEAD_DIM).transpose(0, 2, 1, 3)
    q, k, v = apply_rope(to_heads(q)), apply_rope(to_heads(k)), to_heads(v)
    o = moba_attention(q, k, v).transpose(0, 2, 1, 3).reshape(b, s, ATTN_WIDTH)
    return (o * jax.nn.silu(z)) @ w_out

def conformer_mixer(hn, w_in, b_in, w_dw, b_dw, ln_g, ln_b, w_out, b_out):
    proj = hn @ w_in
    ab = proj[..., :2 * CONV_WIDTH] + b_in
    z = proj[..., 2 * CONV_WIDTH:]
    a, g = jnp.split(ab, 2, axis=-1)
    u = a * jax.nn.sigmoid(g)
    u = lax.conv_general_dilated(
        u, w_dw[:, None, :].astype(u.dtype), window_strides=(1,),
        padding=((CONV_K - 1, 0),), dimension_numbers=('NWC', 'WIO', 'NWC'),
        feature_group_count=CONV_WIDTH) + b_dw
    u = jax.nn.silu(layer_norm(u, ln_g, ln_b))
    return (u * jax.nn.silu(z)) @ w_out + b_out

def setup_inputs(seed: int = 0) -> dict:
    key = jax.random.key(seed)
    ks = jax.random.split(key, 16)
    f32 = jnp.float32
    nrm = lambda k, shape, scale: jax.random.normal(k, shape, f32) * scale
    return {
        "x": nrm(ks[0], (BATCH, SEQ, D_MODEL), 1.0),
        "pre_norm_g": 1.0 + nrm(ks[1], (DEPTH, D_MODEL), 0.05),
        "post_norm_g": 1.0 + nrm(ks[2], (DEPTH, D_MODEL), 0.05),
        "attn_w_in": nrm(ks[3], (N_ATTN_LAYERS, D_MODEL, 4 * ATTN_WIDTH), D_MODEL ** -0.5),
        "attn_w_out": nrm(ks[4], (N_ATTN_LAYERS, ATTN_WIDTH, D_MODEL), ATTN_WIDTH ** -0.5),
        "conv_w_in": nrm(ks[5], (N_CONV_LAYERS, D_MODEL, 3 * CONV_WIDTH), D_MODEL ** -0.5),
        "conv_b_in": nrm(ks[6], (N_CONV_LAYERS, 2 * CONV_WIDTH), 0.02),
        "conv_w_dw": nrm(ks[7], (N_CONV_LAYERS, CONV_K, CONV_WIDTH), CONV_K ** -0.5),
        "conv_b_dw": nrm(ks[8], (N_CONV_LAYERS, CONV_WIDTH), 0.02),
        "conv_ln_g": 1.0 + nrm(ks[9], (N_CONV_LAYERS, CONV_WIDTH), 0.05),
        "conv_ln_b": nrm(ks[10], (N_CONV_LAYERS, CONV_WIDTH), 0.02),
        "conv_w_out": nrm(ks[11], (N_CONV_LAYERS, CONV_WIDTH, D_MODEL), CONV_WIDTH ** -0.5),
        "conv_b_out": nrm(ks[12], (N_CONV_LAYERS, D_MODEL), 0.02),
    }

def reference(x, pre_norm_g, post_norm_g, attn_w_in, attn_w_out, conv_w_in, conv_b_in,
              conv_w_dw, conv_b_dw, conv_ln_g, conv_ln_b, conv_w_out, conv_b_out):
    for i in range(DEPTH):
        hn = rms_norm(x, pre_norm_g[i])
        li = i // N_MIXERS
        if i % N_MIXERS == 0:
            y = moba_mixer(hn, attn_w_in[li], attn_w_out[li])
        else:
            y = conformer_mixer(hn, conv_w_in[li], conv_b_in[li], conv_w_dw[li], conv_b_dw[li],
                                conv_ln_g[li], conv_ln_b[li], conv_w_out[li], conv_b_out[li])
        x = x + rms_norm(y, post_norm_g[i])
    return x


_drawn_inputs = setup_inputs


def setup_inputs(seed=0):
    import zlib

    import numpy as np

    out = dict(_drawn_inputs(seed))
    spreads = {}
    factors = {'conv_b_in': 4.332, 'conv_ln_b': 4.847}
    for name, (base, spread) in spreads.items():
        noise = np.random.default_rng([zlib.crc32(name.encode()), seed]).standard_normal(out[name].shape)
        drawn = base * np.exp(spread * noise) if base else spread * noise
        out[name] = __import__('jax').numpy.asarray(drawn.astype(out[name].dtype))
    for name, factor in factors.items():
        out[name] = (out[name] * factor).astype(out[name].dtype)
    return out
```

```python
import numpy as np
from contextlib import ExitStack

import concourse.bass as bass
from concourse import mybir

P = 128
SEQ = 256
D = 2048
MT = SEQ // P
KT = D // P
NCOL = 512
SL_K = 2
SLICES = KT // SL_K
RING = 4
LOADS = 4
G = 4
NG = D // NCOL
HALF = 64
TAPS = 31
PAD = TAPS - 1
UW = PAD + SEQ
SCALE = float(P) ** -0.5
RMS_EPS = 1e-6
LN_EPS = 1e-5

S_QKVZ = 0
S_OUT0 = S_QKVZ + 4 * NG * SLICES
S_AG = S_OUT0 + NG * SLICES
S_Z = S_AG + 2 * NG * SLICES
S_OUT1 = S_Z + NG * SLICES

V_PRE0, V_PRE1, V_BA, V_BG, V_BDW, V_LNG, V_LNB = range(0, 7 * KT, KT)
NVEC = 7 * KT
ROWS_AT = (8, 11, 15, 25)
DW_ROWS = TAPS * KT // 4


def build(nc, x, pre_g, post_g, w_in0, w_out0, w_in1, b_in, w_dw, b_dw, ln_g, ln_b, w_out1, b_out,
          rope_cos, rope_sin, identity, causal, out):
    f32, f32r = mybir.dt.float32, mybir.dt.float32r
    ALU, ACT, AX = mybir.AluOpType, mybir.ActivationFunctionType, mybir.AxisListType

    ctx = ExitStack()
    with ctx:
        def sem(name):
            return ctx.enter_context(nc.semaphore(name))

        arena = ctx.enter_context(nc.sbuf_tensor("arena", [P, 207 * 256], f32))
        KB = 1024
        base = nc.sbuf_base - 207 * KB

        def at(name, offset, shape, dt=f32):
            size = 4
            for n in shape[1:]:
                size *= n
            assert offset + size <= 207 * KB, name
            return nc.alloc_sbuf_tensor_at(name, shape, dt, offset=base + offset)

        raw = at("raw", 0, [P, LOADS, 4, NCOL])
        w_hi = at("w_hi", 32 * KB, [P, RING, SL_K, NCOL], f32r)
        w_lo = at("w_lo", 48 * KB, [P, RING, SL_K, NCOL], f32r)
        xrow = at("xrow", 64 * KB, [P, MT, D])
        A = 80 * KB
        xT_hi = at("xT_hi", A, [P, KT, SEQ], f32r)
        xT_lo = at("xT_lo", A + 16 * KB, [P, KT, SEQ], f32r)
        gpost0 = at("gpost0", A, [P, D])
        B = 112 * KB
        uT_hi = at("uT_hi", B, [P, KT, SEQ], f32r)
        uT_lo = at("uT_lo", B + 16 * KB, [P, KT, SEQ], f32r)
        c_row = at("c_row", B, [P, MT, D])
        z_row1 = at("z_row1", B + 16 * KB, [P, MT, D])
        y1 = at("y1", B, [P, MT, D])
        gpost1 = at("gpost1", B + 16 * KB, [P, D])
        bout = at("bout", B + 24 * KB, [P, D])
        Dr = 144 * KB
        q_row = at("q_row", Dr, [P, MT, NCOL])
        k_row = at("k_row", Dr + 4 * KB, [P, MT, NCOL])
        rope_t = at("rope_t", Dr + 8 * KB, [P, MT, NCOL])
        qT = at("qT", Dr + 12 * KB, [P, G, SEQ])
        kT = at("kT", Dr + 16 * KB, [P, G, SEQ])
        probs = at("probs", Dr + 20 * KB, [P, G, 3 * P])
        junk0 = at("junk0", Dr + 12 * KB, [P, D])
        y0 = at("y0", Dr, [P, MT, D])
        a_row = at("a_row", Dr, [P, MT, NCOL])
        g_row = at("g_row", Dr + 4 * KB, [P, MT, NCOL])
        sig = at("sig", Dr + 8 * KB, [P, G, SEQ])
        u_pad = at("u_pad", Dr + 12 * KB, [P, KT, UW])
        junk2 = at("junk2", B, [P, D])
        yg1 = at("yg1", A, [P, MT, D])
        vT_hi = at("vT_hi", Dr, [P, KT, SEQ], f32r)
        vT_lo = at("vT_lo", Dr + 16 * KB, [P, KT, SEQ], f32r)
        C = 176 * KB
        v_row = at("v_row", C, [P, MT, NCOL])
        z_row = at("z_row", C + 4 * KB, [P, MT, NCOL])
        u_row = at("u_row", C + 8 * KB, [P, MT, NCOL])
        pT = at("pT", C + 12 * KB, [P, G, 3 * P])
        cT = at("cT", C, [P, KT, SEQ])
        junk1 = at("junk1", C + 16 * KB, [P, NCOL])
        t_buf = at("t_buf", C + 16 * KB, [P, G, SEQ])
        vec_rows = at("vec_rows", C, [NVEC, P])
        dw_rows = at("dw_rows", C + 512, [DW_ROWS, 4, P])
        vec = at("vec", C + 20 * KB, [P, NVEC])
        taps = at("taps", C + 20 * KB + 512, [P, TAPS * KT])
        cos_t = at("cos_t", C + 22 * KB + 512, [P, MT, P])
        sin_t = at("sin_t", C + 23 * KB + 512, [P, MT, P])
        ident = at("ident", C + 24 * KB + 512, [P, P])
        mask = at("mask", C + 25 * KB, [P, P])
        small = at("small", C + 25 * KB + 512, [P, 128])
        ssq = small[:, 2:10].rearrange("p (m n) -> p m n", m=MT)
        mean_sq = small[:, 10:12]
        mean_sum = small[:, 0:2]
        rms = [small[:, 12 + 2 * i:14 + 2 * i] for i in range(4)]
        row_max = small[:, 20:28].rearrange("p (h m) -> p h m", h=G)
        neg_max = small[:, 28:36].rearrange("p (h m) -> p h m", h=G)
        row_sum = small[:, 36:44].rearrange("p (h m) -> p h m", h=G)
        inv_sum = small[:, 44:52].rearrange("p (h m) -> p h m", h=G)
        bn = small[:, 52:100].rearrange("p (m n s) -> p m n s", m=MT, n=NG)
        mv = small[:, 100:104].rearrange("p (m s) -> p m s", m=MT)
        rstd = small[:, 104:106]
        var_eps = small[:, 106:108]
        m_half = small[:, 108:110]

        acc = ctx.enter_context(nc.psum_tensor("acc", [P, 2, MT, NCOL], f32))
        X = [ctx.enter_context(nc.psum_tensor(f"X{i}", [P, NCOL], f32)) for i in range(4)]

        raw_ready = [sem(f"raw_ready{i}") for i in range(LOADS)]
        hi_ready = [sem(f"hi_ready{i}") for i in range(RING)]
        lo_ready = [sem(f"lo_ready{i}") for i in range(RING)]
        w_used = [sem(f"w_used{i}") for i in range(RING)]
        rows_out = sem("rows_out")
        acc_read = sem("acc_read")
        x_in = [sem(f"x_in{i}") for i in range(NG)]
        ident_in = sem("ident_in")
        vec_in = sem("vec_in")
        dw_in = sem("dw_in")
        rope_in = sem("rope_in")
        gpost0_in = sem("gpost0_in")
        bcast1_in = sem("bcast1_in")
        vec_T = sem("vec_T")
        vec_ready = sem("vec_ready")
        const_set = sem("const_set")
        xT_done = sem("xT_done")
        xhi_ready = sem("xhi_ready")
        xlo_ready = sem("xlo_ready")
        ssq_ready = sem("ssq_ready")
        ms_ready = sem("ms_ready")
        rms_ready = sem("rms_ready")
        rope_step = sem("rope_step")
        qT_done, kT_done = sem("qT_done"), sem("kT_done")
        qT_ready, kT_ready = sem("qT_ready"), sem("kT_ready")
        s_done = sem("s_done")
        max_ready = sem("max_ready")
        negmax_ready = sem("negmax_ready")
        p_ready = sem("p_ready")
        pT_done = sem("pT_done")
        pT_ready = sem("pT_ready")
        inv_ready = sem("inv_ready")
        pv_done = sem("pv_done")
        u_ready = sem("u_ready")
        uT_done = sem("uT_done")
        uhi_ready, ulo_ready = sem("uhi_ready"), sem("ulo_ready")
        sum_ready = sem("sum_ready")
        x1_ready = sem("x1_ready")
        agT_done = sem("agT_done")
        sig_ready = sem("sig_ready")
        pad_set = sem("pad_set")
        gated = sem("gated")
        conv_step = sem("conv_step")
        conv_done = sem("conv_done")
        cR_done = sem("cR_done")
        c_ready = sem("c_ready")
        bn_ready = sem("bn_ready")
        mv_ready = sem("mv_ready")
        var_ready = sem("var_ready")
        rstd_ready = sem("rstd_ready")
        norm_ready = sem("norm_ready")
        fT_done = sem("fT_done")
        silu_ready = sem("silu_ready")
        t_ready = sem("t_ready")
        vhi_ready, vlo_ready = sem("vhi_ready"), sem("vlo_ready")
        y_ready = sem("y_ready")
        yg_ready = sem("yg_ready")
        o_ready = sem("o_ready")
        stored = sem("stored")

        block = ctx.enter_context(nc.Block())

        def cols(w):
            return w.rearrange("(t p) n -> p t n", p=P)

        def rounds(first, it, per, s):
            return it * (per // RING) + (first + s) // RING + 1

        def rd(t, slot):
            return t[:, slot].bitcast(f32)

        @block.sync
        def _(sp):
            def load(first, it, per, j, w, col):
                u = first // 2 + j
                slot = u % LOADS
                if first or not isinstance(it, int) or it or j >= LOADS:
                    for i in (0, 1):
                        sp.wait_ge(lo_ready[(2 * u + i) % RING],
                                   rounds(first - 2 * LOADS, it, per, 2 * j + i))
                kg = j % 4
                sp.dma_start(raw[:, slot], cols(w)[:, 4 * kg:4 * kg + 4, bass.ds(col, NCOL)]
                             ).then_inc(raw_ready[slot], 16)

            xv = x.rearrange("b (m p) n -> p (b m) n", p=P)
            sp.dma_start(ident[:], identity).then_inc(ident_in, 16)
            sp.dma_start(xrow[:, :, 0:NCOL], xv[:, :, 0:NCOL]).then_inc(x_in[0], 16)
            for v, src in ((V_PRE0, pre_g[0]), (V_PRE1, pre_g[1]), (V_BA, b_in[0, 0:D]),
                           (V_BG, b_in[0, D:2 * D]), (V_BDW, b_dw[0]), (V_LNG, ln_g[0]), (V_LNB, ln_b[0])):
                sp.dma_start(vec_rows[v:v + KT, :], src.rearrange("(t c) -> t c", c=P)).then_inc(vec_in, 16)
            for n in range(1, NG):
                c = slice(n * NCOL, (n + 1) * NCOL)
                sp.dma_start(xrow[:, :, c], xv[:, :, c]).then_inc(x_in[n], 16)
                if n == 1:
                    for j in range(2):
                        load(S_QKVZ, 0, 32, j, w_in0[0], 0)
            sp.dma_start(dw_rows[:], w_dw[0].rearrange("k (t c) -> (k t) c", c=P)
                         .rearrange("(q r) c -> r q c", r=DW_ROWS)).then_inc(dw_in, 16)
            sp.dma_start(cos_t[:], rope_cos).then_inc(rope_in, 16)
            sp.dma_start(sin_t[:], rope_sin).then_inc(rope_in, 16)
            sp.dma_start(mask[:], causal).then_inc(rope_in, 16)

            for j in range(2, 16):
                load(S_QKVZ, 0, 32, j, w_in0[0], (j // 4) * D)
            with sp.Fori(1, NG) as g:
                for j in range(16):
                    load(S_QKVZ, g, 32, j, w_in0[0], g * NCOL + (j // 4) * D)
            for j in range(16):
                load(S_OUT0, 0, 32, j, w_out0[0], (j // 4) * NCOL)
                if j == 3:
                    sp.wait_ge(w_used[RING - 1], rounds(S_OUT0, 0, 0, -1))
                    sp.dma_start(gpost0[:], post_g[0:1].to_broadcast([P, D])).then_inc(gpost0_in, 16)
            with sp.Fori(0, NG) as j4:
                for j in range(8):
                    load(S_AG, j4, 16, j, w_in1[0], j4 * NCOL + (j // 4) * D)
            with sp.Fori(0, NG) as n:
                for j in range(4):
                    load(S_Z, n, 8, j, w_in1[0], n * NCOL + 2 * D)
            for j in range(16):
                load(S_OUT1, 0, 32, j, w_out1[0], (j // 4) * NCOL)
                if j == 5:
                    sp.wait_ge(fT_done, NG)
                    sp.dma_start(gpost1[:], post_g[1:2].to_broadcast([P, D])).then_inc(bcast1_in, 16)
                    sp.dma_start(bout[:], b_out[0:1].to_broadcast([P, D])).then_inc(bcast1_in, 16)
            ov = out.rearrange("b (m p) n -> p (b m) n", p=P)
            for n in range(NG):
                c = slice(n * NCOL, (n + 1) * NCOL)
                sp.wait_ge(o_ready, n + 1)
                sp.dma_start(ov[:, :, c], xrow[:, :, c]).then_inc(stored, 16)
            sp.wait_ge(stored, 16 * NG)

        @block.tensor
        def _(pe):
            def slice_products(first, it, per, s, hi, lo):
                slot = s % RING
                par = ((first + s) // SLICES) % 2
                pe.wait_ge(lo_ready[slot], rounds(first, it, per, s))
                for i in range(SL_K):
                    k = SL_K * (s % SLICES) + i
                    for m in range(MT):
                        rows = slice(m * P, (m + 1) * P)
                        a = acc[:, par, m]
                        nc.tensor.matmul(a, hi[:, k, rows], w_hi[:, slot, i], start=(k == 0), stop=False)
                        nc.tensor.matmul(a, hi[:, k, rows], w_lo[:, slot, i], start=False, stop=False)
                        last = nc.tensor.matmul(a, lo[:, k, rows], w_hi[:, slot, i], start=False,
                                                stop=(k == KT - 1))
                last.then_inc(w_used[slot], 1)

            def pair_T(rows, bank, tile):
                for i in range(2):
                    for m in range(MT):
                        last = nc.tensor.transpose(bank[:, i * SEQ + m * P:i * SEQ + (m + 1) * P],
                                                   rows[:, m, (tile + i) * P:(tile + i + 1) * P], ident[:])
                return last

            def acc_free(b):
                o = b - 2
                if 0 <= o < 32:
                    pe.wait_ge(rows_out, o + 1)
                if 16 <= o < 20:
                    pe.wait_ge(acc_read, o - 15)
                if o >= 32:
                    pe.wait_ge(acc_read, o - 27)

            pe.wait_ge(ident_in, 16)
            for n in range(NG):
                pe.wait_ge(x_in[n], 16)
                if n == 1:
                    pe.wait_ge(vec_ready, 1)
                if n >= 2:
                    pe.wait_ge(xlo_ready, n - 1)
                pair_T(xrow, X[2 * (n % 2)], 4 * n)
                pair_T(xrow, X[2 * (n % 2) + 1], 4 * n + 2).then_inc(xT_done, 1)
                if n == 0:
                    pe.wait_ge(vec_in, 16 * 7)
                    nc.tensor.transpose(X[2][:, 0:NVEC], vec_rows[:], ident[0:NVEC, 0:NVEC]).then_inc(vec_T, 1)

            def scores(g, h):
                s = X[h]
                nc.tensor.matmul(s[:, 0:P], qT[:, h, 0:P], kT[:, h, 0:P], start=True, stop=False)
                nc.tensor.matmul(s[:, 0:P], ident[:], mask[:], start=False, stop=True)
                nc.tensor.matmul(s[:, P:2 * P], qT[:, h, P:SEQ], kT[:, h, 0:P], start=True, stop=True)
                nc.tensor.matmul(s[:, 2 * P:3 * P], qT[:, h, P:SEQ], kT[:, h, P:SEQ], start=True, stop=False)
                nc.tensor.matmul(s[:, 2 * P:3 * P], ident[:], mask[:], start=False, stop=True
                                 ).then_inc(s_done, 1)

            def probs_T(g, h):
                pe.wait_ge(p_ready, G * g + h + 1)
                for i in range(3):
                    last = nc.tensor.transpose(X[h][:, i * P:(i + 1) * P], probs[:, h, i * P:(i + 1) * P], ident[:])
                last.then_inc(pT_done, 1)

            def values(g):
                pe.wait_ge(pT_ready, G * (g + 1))
                pe.wait_ge(rows_out, 4 * g + 3)
                for h in range(G):
                    c = slice(h * P, (h + 1) * P)
                    nc.tensor.matmul(X[0][:, c], pT[:, h, 0:P], v_row[:, 0, c], start=True, stop=True)
                    nc.tensor.matmul(X[1][:, c], pT[:, h, P:2 * P], v_row[:, 0, c], start=True, stop=False)
                    last = nc.tensor.matmul(X[1][:, c], pT[:, h, 2 * P:3 * P], v_row[:, 1, c],
                                            start=False, stop=True)
                last.then_inc(pv_done, 1)

            def gated_T(g):
                pe.wait_ge(u_ready, g + 1)
                pair_T(u_row, X[2], 0)
                pair_T(u_row, X[3], 2).then_inc(uT_done, 1)

            def group(g, first):
                for s in range(4 * SLICES):
                    if s % SLICES == 0 and not (first and s < 2 * SLICES):
                        pe.wait_ge(rows_out, 4 * g + s // SLICES - 1)
                    if first and s % 2 == 0 and s < SLICES:
                        pe.wait_ge(xlo_ready, s // 2 + 1)
                    slice_products(S_QKVZ, g, 32, s, xT_hi, xT_lo)
                    if s == 3 and not first:
                        gated_T(g - 1)
                    if s == 4 and first:
                        pe.wait_ge(dw_in, 16)
                        for q in range(4):
                            last = nc.tensor.transpose(X[0][:, q * DW_ROWS:(q + 1) * DW_ROWS], dw_rows[:, q, :],
                                                       ident[0:DW_ROWS, 0:DW_ROWS])
                        last.then_inc(vec_T, 1)
                    if s == 14:
                        pe.wait_ge(rope_step, 6 * g + 3)
                        if first:
                            pe.wait_ge(vec_ready, 2)
                        else:
                            pe.wait_ge(u_ready, g)
                        pair_T(q_row, X[0], 0)
                        pair_T(q_row, X[1], 2).then_inc(qT_done, 1)
                    if s == 20:
                        pe.wait_ge(rope_step, 6 * g + 6)
                        if not first:
                            pe.wait_ge(ulo_ready, g)
                        pair_T(k_row, X[2], 0)
                        pair_T(k_row, X[3], 2).then_inc(kT_done, 1)
                    if s == 22:
                        if first:
                            pe.wait_ge(rope_in, 48)
                        pe.wait_ge(qT_ready, g + 1)
                        pe.wait_ge(kT_ready, g + 1)
                        for h in range(G):
                            scores(g, h)
                    if s in (26, 27):
                        for h in (0, 1) if s == 26 else (2, 3):
                            probs_T(g, h)
                    if s == 30:
                        values(g)

            group(0, True)
            with pe.Fori(1, NG) as g:
                group(g, False)

            for s in range(4 * SLICES):
                if s % SLICES == 0:
                    acc_free(16 + s // SLICES)
                if s % 2 == 0 and s < SLICES:
                    pe.wait_ge(ulo_ready, s // 2 + 1)
                slice_products(S_OUT0, 0, 0, s, uT_hi, uT_lo)
                if s == 3:
                    gated_T(NG - 1)

            acc_free(20)
            for n in range(NG):
                pe.wait_ge(x1_ready, n + 1)
                if n == 0:
                    pe.wait_ge(ulo_ready, NG)
                if n >= 2:
                    pe.wait_ge(xlo_ready, NG + n - 1)
                pair_T(xrow, X[2 * (n % 2)], 4 * n)
                pair_T(xrow, X[2 * (n % 2) + 1], 4 * n + 2).then_inc(xT_done, 1)
                if n >= 1:
                    pe.wait_ge(xlo_ready, NG + n)
                    for s in (2 * n - 2, 2 * n - 1):
                        slice_products(S_AG, 0, 16, s, xT_hi, xT_lo)
            pe.wait_ge(xlo_ready, 2 * NG)

            def conv_input_T(j, half):
                if half == 0:
                    pe.wait_ge(rows_out, 20 + 2 * (j + 1))
                    if not (isinstance(j, int) and j == 0):
                        pe.wait_ge(gated, 2 * j)
                else:
                    pe.wait_ge(gated, 2 * j + 1)
                pair_T(a_row, X[0], 2 * half)
                pair_T(g_row, X[1], 2 * half).then_inc(agT_done, 1)

            def halves(j, first):
                for s in range(6 if first else 0, 2 * SLICES):
                    if s % SLICES == 0:
                        if first:
                            acc_free(20 + s // SLICES)
                        else:
                            pe.wait_ge(rows_out, 20 + 2 * j + s // SLICES - 1)
                    slice_products(S_AG, j, 16, s, xT_hi, xT_lo)
                    if s in (1, 9) and not first:
                        conv_input_T(j - 1, s // SLICES)

            halves(0, True)
            with pe.Fori(1, NG) as j:
                halves(j, False)

            def conv_rows(j):
                pe.wait_ge(conv_done, G * (j + 1))
                for m in range(MT):
                    if j or m:
                        pe.wait_ge(c_ready, MT * j + m)
                    for c in range(G):
                        last = nc.tensor.transpose(X[3][:, c * P:(c + 1) * P],
                                                   cT[:, G * j + c, m * P:(m + 1) * P], ident[:])
                    last.then_inc(cR_done, 1)

            def final_T(n):
                pe.wait_ge(norm_ready, n + 1)
                pe.wait_ge(rows_out, 28 + n + 1)
                if n:
                    pe.wait_ge(silu_ready, n)
                    pe.wait_ge(t_ready, n)
                for b in range(2):
                    pair_T(c_row, X[b], 4 * n + 2 * b)
                    last = pair_T(z_row1, X[2 + b], 4 * n + 2 * b)
                last.then_inc(fT_done, 1)

            for s in range(4 * SLICES):
                if s % SLICES == 0:
                    acc_free(28 + s // SLICES)
                slice_products(S_Z, 0, 0, s, xT_hi, xT_lo)
                if s in (1, 9):
                    conv_input_T(NG - 1, s // SLICES)
                if s in ROWS_AT:
                    conv_rows(ROWS_AT.index(s))
                if s in (28, 30):
                    final_T((s - 28) // 2)

            for s in range(4 * SLICES):
                if s % SLICES == 0:
                    acc_free(32 + s // SLICES)
                if s < SLICES and s % 2 == 0:
                    pe.wait_ge(vlo_ready, s // 2 + 1)
                slice_products(S_OUT1, 0, 0, s, vT_hi, vT_lo)
                if s in (0, 2):
                    final_T(2 + s // 2)

        @block.scalar
        def _(act):
            def high(first, it, per, s):
                u = first // 2 + s // 2
                slot = s % RING
                act.wait_ge(raw_ready[u % LOADS], 16 * (it * (per // 2 // LOADS) + u // LOADS + 1))
                if first or not isinstance(it, int) or it or s >= RING:
                    act.wait_ge(w_used[slot], rounds(first - RING, it, per, s))
                half = s % 2
                nc.scalar.activation(w_hi[:, slot], raw[:, u % LOADS, 2 * half:2 * half + 2], ACT.Copy
                                     ).then_inc(hi_ready[slot], 1)

            def block_rows(first, it, per, s, dst, scale, func=ACT.Copy):
                act.wait_ge(w_used[RING - 1], rounds(first, it, per, s))
                par = ((first + s) // SLICES) % 2
                for m in range(MT):
                    last = nc.scalar.activation(dst[:, m], acc[:, par, m], func, scale=scale[:, m:m + 1])
                last.then_inc(rows_out, 1)

            def input_high(layer, n, vcol):
                act.wait_ge(xT_done, NG * layer + n + 1)
                for c in range(4):
                    t = 4 * n + c
                    last = nc.scalar.activation(
                        xT_hi[:, t], X[2 * (n % 2) + c // 2][:, (c % 2) * SEQ:(c % 2 + 1) * SEQ], ACT.Copy,
                        scale=vec[:, vcol + t:vcol + t + 1])
                last.then_inc(xhi_ready, 1)

            def squares(junk, row, m, n, before):
                if before:
                    act.wait_ge(ssq_ready, before)
                nc.scalar.activation(junk, row, ACT.Square, accum_out=ssq[:, m, n:n + 1]).then_inc(ssq_ready, 1)

            act.wait_ge(vec_T, 1)
            nc.scalar.activation(vec[:], X[2][:, 0:NVEC], ACT.Copy).then_inc(vec_ready, 1)
            act.wait_ge(vec_ready, 1)
            for n in range(NG):
                input_high(0, n, V_PRE0)
                high(S_QKVZ, 0, 32, n)
            for m in range(MT):
                squares(junk0[:], xrow[:, m], m, 0, m)

            def heads_high(g):
                act.wait_ge(uT_done, g + 1)
                for b in range(2):
                    last = nc.scalar.activation(uT_hi[:, bass.ds(g * 4 + 2 * b, 2)], X[2 + b][:], ACT.Copy)
                last.then_inc(uhi_ready, 1)

            def group_end(s, g):
                if s == 3:
                    if not (isinstance(g, int) and g == 0):
                        act.wait_ge(u_ready, g)
                    block_rows(S_QKVZ, g, 32, 31, z_row, rms[0], ACT.Silu)
                if s == 7:
                    heads_high(g)

            def exponentials(g, h, first):
                if h == 0 and not first:
                    act.wait_ge(pT_done, G * g)
                act.wait_ge(negmax_ready, G * g + h + 1)
                for m in range(MT):
                    c = slice(0, P) if m == 0 else slice(P, 3 * P)
                    last = nc.scalar.activation(probs[:, h, c], X[h][:, c], ACT.Exp, bias=neg_max[:, h, m:m + 1],
                                                scale=SCALE, accum_out=row_sum[:, h, m:m + 1])
                last.then_inc(p_ready, 1)

            def group(g, first):
                for s in range(4 * SLICES):
                    if not (first and s < RING):
                        high(S_QKVZ, g, 32, s)
                    if not first:
                        group_end(s, g - 1)
                    if s == 8 and first:
                        act.wait_ge(vec_T, 2)
                        nc.scalar.activation(taps[:], X[0][:, 0:TAPS * KT], ACT.Copy).then_inc(vec_ready, 1)
                        act.wait_ge(rms_ready, 1)
                    if s == 11:
                        block_rows(S_QKVZ, g, 32, 7, q_row, rms[0])
                    if s == 18:
                        act.wait_ge(qT_done, g + 1)
                        for b in range(2):
                            last = nc.scalar.activation(qT[:, 2 * b:2 * b + 2], X[b][:], ACT.Copy)
                        last.then_inc(qT_ready, 1)
                    if s == 19:
                        block_rows(S_QKVZ, g, 32, 15, k_row, rms[0])
                    if s == 24:
                        act.wait_ge(kT_done, g + 1)
                        for b in range(2):
                            last = nc.scalar.activation(kT[:, 2 * b:2 * b + 2], X[2 + b][:], ACT.Copy)
                        last.then_inc(kT_ready, 1)
                    if s == 27:
                        if not first:
                            act.wait_ge(pv_done, g)
                        block_rows(S_QKVZ, g, 32, 23, v_row, rms[0])
                    if s in (26, 27, 28, 29):
                        exponentials(g, s - 26, first)

            group(0, True)
            with act.Fori(1, NG) as g:
                group(g, False)

            def out0_squares(n):
                act.wait_ge(w_used[RING - 1], rounds(S_OUT0, 0, 0, 8 * n + 7))
                for m in range(MT):
                    squares(junk1[:], acc[:, n % 2, m], m, n, 2 + MT * n + m)
                act.wait_ge(ssq_ready, 2 + MT * (n + 1))
                act.sem_inc(rows_out, 1)

            for s in range(4 * SLICES):
                high(S_OUT0, 0, 0, s)
                group_end(s, NG - 1)
                if s % SLICES == 3 and s > SLICES:
                    out0_squares(s // SLICES - 1)
            for s in range(RING):
                high(S_AG, 0, 16, s)
            out0_squares(NG - 1)
            input_high(1, 0, V_PRE1)
            input_high(1, 1, V_PRE1)
            high(S_AG, 0, 16, 4)
            high(S_AG, 0, 16, 5)
            input_high(1, 2, V_PRE1)
            high(S_AG, 0, 16, 6)
            high(S_AG, 0, 16, 7)
            input_high(1, 3, V_PRE1)
            for m in range(MT):
                squares(junk2[:], xrow[:, m], m, 0, 10 + m)

            def gate_sigmoid(j, half):
                act.wait_ge(agT_done, 2 * j + half + 1)
                for c in range(2):
                    t = 2 * half + c
                    last = nc.scalar.activation(sig[:, t], X[1][:, c * SEQ:(c + 1) * SEQ], ACT.Sigmoid,
                                                bias=vec[:, bass.ds(V_BG + j * 4 + t, 1)])
                last.then_inc(sig_ready, 1)

            def halves(j, first):
                for s in range(8 if first else 0, 2 * SLICES):
                    high(S_AG, j, 16, s)
                    if s == 3 and not first:
                        block_rows(S_AG, j - 1, 16, 15, g_row, rms[2])
                    if s in (5, 13) and not first:
                        gate_sigmoid(j - 1, s // SLICES)
                    if s == 14:
                        if first:
                            act.wait_ge(rms_ready, 3)
                        block_rows(S_AG, j, 16, 7, a_row, rms[2])

            halves(0, True)
            with act.Fori(1, NG) as j:
                halves(j, False)

            for s in range(4 * SLICES):
                high(S_Z, 0, 0, s)
                if s == 3:
                    block_rows(S_AG, NG - 1, 16, 15, g_row, rms[2])
                if s in (5, 13):
                    gate_sigmoid(NG - 1, s // SLICES)
                if s % SLICES == 3 and s > SLICES:
                    n = s // SLICES - 1
                    block_rows(S_Z, 0, 0, 8 * n + 7, z_row1[:, :, n * NCOL:(n + 1) * NCOL], rms[2], ACT.Silu)
                for j in range(NG):
                    for m in range(MT):
                        if s == min(ROWS_AT[j] + 3 + m, 31):
                            act.wait_ge(cR_done, MT * j + m + 1)
                            nc.scalar.activation(c_row[:, m, j * NCOL:(j + 1) * NCOL], X[3][:], ACT.Copy
                                                 ).then_inc(c_ready, 1)

            def affine_silu(n):
                act.wait_ge(fT_done, n + 1)
                if n:
                    act.wait_ge(vlo_ready, n)
                for c in range(4):
                    t = 4 * n + c
                    last = nc.scalar.activation(t_buf[:, c], X[c // 2][:, (c % 2) * SEQ:(c % 2 + 1) * SEQ], ACT.Silu,
                                                scale=vec[:, V_LNG + t:V_LNG + t + 1],
                                                bias=vec[:, V_LNB + t:V_LNB + t + 1])
                last.then_inc(silu_ready, 1)

            def final_high(n):
                act.wait_ge(t_ready, n + 1)
                nc.scalar.activation(vT_hi[:, 4 * n:4 * n + 4], t_buf[:], ACT.Copy).then_inc(vhi_ready, 1)

            def out1_squares(n):
                act.wait_ge(y_ready, n + 1)
                for m in range(MT):
                    squares(junk1[:], y1[:, m, n * NCOL:(n + 1) * NCOL], m, n, 12 + MT * n + m)

            for s in range(4 * SLICES):
                high(S_OUT1, 0, 0, s)
                if s in (0, 2, 4, 6):
                    affine_silu(s // 2)
                if s in (1, 3, 5, 7):
                    final_high(s // 2)
                if s == 3:
                    block_rows(S_Z, 0, 0, 31, z_row1[:, :, 3 * NCOL:4 * NCOL], rms[2], ACT.Silu)
                if s % SLICES == 4 and s > SLICES:
                    out1_squares(s // SLICES - 1)
            out1_squares(NG - 1)

        @block.vector
        def _(dve):
            def low(first, it, per, s):
                u = first // 2 + s // 2
                slot = s % RING
                half = s % 2
                dve.wait_ge(hi_ready[slot], rounds(first, it, per, s))
                nc.vector.tensor_tensor(w_lo[:, slot], raw[:, u % LOADS, 2 * half:2 * half + 2], rd(w_hi, slot),
                                        ALU.subtract).then_inc(lo_ready[slot], 1)

            def input_low(layer, n, vcol):
                dve.wait_ge(xhi_ready, NG * layer + n + 1)
                for c in range(4):
                    t = 4 * n + c
                    last = nc.vector.scalar_tensor_tensor(
                        out=xT_lo[:, t], in0=X[2 * (n % 2) + c // 2][:, (c % 2) * SEQ:(c % 2 + 1) * SEQ],
                        scalar=vec[:, vcol + t:vcol + t + 1], in1=xT_hi[:, t].bitcast(f32),
                        op0=ALU.mult, op1=ALU.subtract)
                last.then_inc(xlo_ready, 1)

            def mean_square(first):
                nc.vector.tensor_scalar(mean_sq, first, 1.0 / D, RMS_EPS, ALU.mult, ALU.add).then_inc(ms_ready, 1)

            for n in range(NG):
                input_low(0, n, V_PRE0)
                low(S_QKVZ, 0, 32, n)
            dve.wait_ge(ssq_ready, 2)
            mean_square(ssq[:, :, 0])

            def gate_outputs(g):
                dve.wait_ge(pv_done, g + 1)
                dve.wait_ge(rows_out, 4 * (g + 1))
                dve.wait_ge(inv_ready, g + 1)
                for m in range(MT):
                    for h in range(G):
                        c = slice(h * P, (h + 1) * P)
                        last = nc.vector.scalar_tensor_tensor(
                            out=u_row[:, m, c], in0=X[m][:, c], scalar=inv_sum[:, h, m:m + 1], in1=z_row[:, m, c],
                            op0=ALU.mult, op1=ALU.mult)
                last.then_inc(u_ready, 1)

            def heads_low(g):
                dve.wait_ge(uhi_ready, g + 1)
                for b in range(2):
                    t = bass.ds(g * 4 + 2 * b, 2)
                    last = nc.vector.tensor_tensor(uT_lo[:, t], X[2 + b][:].rearrange("p (t r) -> p t r", t=2),
                                                   uT_hi[:, t].bitcast(f32), ALU.subtract)
                last.then_inc(ulo_ready, 1)

            def group_end(s, g):
                if s == 4:
                    gate_outputs(g)
                if s == 7:
                    heads_low(g)

            def maxima(g, h):
                dve.wait_ge(s_done, G * g + h + 1)
                nc.vector.reduce_max(row_max[:, h, 0:1], X[h][:, 0:P], AX.X)
                nc.vector.reduce_max(row_max[:, h, 1:2], X[h][:, P:3 * P], AX.X).then_inc(max_ready, 1)
                dve.wait_ge(max_ready, G * g + h + 1)
                nc.vector.tensor_scalar(neg_max[:, h], row_max[:, h], -SCALE, None, ALU.mult
                                        ).then_inc(negmax_ready, 1)

            def group(g, first):
                for s in range(4 * SLICES):
                    if not (first and s < RING):
                        low(S_QKVZ, g, 32, s)
                    if not first:
                        group_end(s, g - 1)
                    if s in (26, 27):
                        for h in (0, 1) if s == 26 else (2, 3):
                            maxima(g, h)
                    if s in (30, 31):
                        for h in (0, 1) if s == 30 else (2, 3):
                            dve.wait_ge(pT_done, G * g + h + 1)
                            nc.vector.tensor_copy(pT[:, h], X[h][:, 0:3 * P]).then_inc(pT_ready, 1)
                    if s == 31:
                        dve.wait_ge(p_ready, G * g + 4)
                        nc.vector.reciprocal(small[:, 44:52], small[:, 36:44]).then_inc(inv_ready, 1)

            group(0, True)
            with dve.Fori(1, NG) as g:
                group(g, False)

            def out0_rows(n):
                if n == 0:
                    dve.wait_ge(gpost0_in, 16)
                for m in range(MT):
                    dve.wait_ge(ssq_ready, 2 + MT * n + m + 1)
                    c = slice(n * NCOL, (n + 1) * NCOL)
                    last = nc.vector.tensor_tensor(y0[:, m, c], acc[:, n % 2, m], gpost0[:, c], ALU.mult)
                last.then_inc(acc_read, 1)

            for s in range(4 * SLICES):
                low(S_OUT0, 0, 0, s)
                group_end(s, NG - 1)
                if s % SLICES == 3 and s > SLICES:
                    out0_rows(s // SLICES - 1)
            out0_rows(NG - 1)

            def residual(n, r, y, done):
                for m in range(MT):
                    c = slice(n * NCOL, (n + 1) * NCOL)
                    last = nc.vector.scalar_tensor_tensor(
                        out=xrow[:, m, c], in0=y[:, m, c], scalar=rms[r][:, m:m + 1], in1=xrow[:, m, c],
                        op0=ALU.mult, op1=ALU.add)
                last.then_inc(done, 1)

            dve.wait_ge(ssq_ready, 10)
            nc.vector.reduce_sum(mean_sum, ssq, AX.X).then_inc(sum_ready, 1)
            dve.wait_ge(sum_ready, 1)
            mean_square(mean_sum)
            dve.wait_ge(rms_ready, 2)
            dve.wait_ge(acc_read, NG)
            residual(0, 1, y0, x1_ready)
            residual(1, 1, y0, x1_ready)
            input_low(1, 0, V_PRE1)
            residual(2, 1, y0, x1_ready)
            input_low(1, 1, V_PRE1)
            residual(3, 1, y0, x1_ready)
            input_low(1, 2, V_PRE1)
            input_low(1, 3, V_PRE1)
            dve.wait_ge(x1_ready, NG)
            nc.vector.memset(u_pad[:, :, 0:PAD], 0.0).then_inc(pad_set, 1)
            dve.wait_ge(ssq_ready, 12)
            mean_square(ssq[:, :, 0])
            dve.wait_ge(pad_set, 1)

            def conv_input(j, half):
                dve.wait_ge(sig_ready, 2 * j + half + 1)
                for c in range(2):
                    t = 2 * half + c
                    last = nc.vector.scalar_tensor_tensor(
                        out=u_pad[:, j * 4 + t, PAD:UW], in0=X[0][:, c * SEQ:(c + 1) * SEQ],
                        scalar=vec[:, bass.ds(V_BA + j * 4 + t, 1)], in1=sig[:, t], op0=ALU.add, op1=ALU.mult)
                last.then_inc(gated, 1)

            def convolve(j, t):
                tile = j * 4 + t
                part = X[2][:, (t % 2) * SEQ:(t % 2 + 1) * SEQ]
                if t % 2 == 0:
                    dve.wait_ge(gated, 2 * j + t // 2 + 1)
                nc.vector.tensor_scalar(part, u_pad[:, tile, 0:SEQ], taps[:, bass.ds(tile, 1)],
                                        vec[:, bass.ds(V_BDW + tile, 1)], ALU.mult, ALU.add
                                        ).then_inc(conv_step, 1)
                for k in range(1, TAPS):
                    dve.wait_ge(conv_step, tile * (TAPS - 1) + k)
                    nc.vector.scalar_tensor_tensor(
                        out=cT[:, tile] if k == TAPS - 1 else part, in0=u_pad[:, tile, k:k + SEQ],
                        scalar=taps[:, bass.ds(k * KT + tile, 1)], in1=part, op0=ALU.mult, op1=ALU.add
                        ).then_inc(conv_done if k == TAPS - 1 else conv_step, 1)

            with dve.Fori(0, NG) as j:
                conv_input(j, 0)
                convolve(j, 0)
                conv_input(j, 1)
                for t in range(1, G):
                    convolve(j, t)

            for n in range(NG):
                for m in range(MT):
                    dve.wait_ge(c_ready, MT * n + m + 1)
                    nc.vector.bn_stats(bn[:, m, n], c_row[:, m, n * NCOL:(n + 1) * NCOL]).then_inc(bn_ready, 1)
            dve.wait_ge(bn_ready, MT * NG)
            for m in range(MT):
                nc.vector.bn_aggr(mv[:, m], bn[:, m]).then_inc(mv_ready, 1)
            dve.wait_ge(mv_ready, MT)
            nc.vector.tensor_scalar(var_eps, mv[:, :, 1], LN_EPS, None, ALU.add).then_inc(var_ready, 1)
            dve.wait_ge(rstd_ready, 1)
            for n in range(NG):
                for m in range(MT):
                    c = c_row[:, m, n * NCOL:(n + 1) * NCOL]
                    last = nc.vector.tensor_scalar(c, c, mv[:, m, 0:1], rstd[:, m:m + 1], ALU.subtract, ALU.mult)
                last.then_inc(norm_ready, 1)

            for n in range(NG):
                dve.wait_ge(silu_ready, n + 1)
                for b in range(2):
                    part = t_buf[:, 2 * b:2 * b + 2]
                    last = nc.vector.tensor_tensor(part, part, X[2 + b][:].rearrange("p (t r) -> p t r", t=2), ALU.mult)
                last.then_inc(t_ready, 1)
                dve.wait_ge(vhi_ready, n + 1)
                nc.vector.tensor_tensor(vT_lo[:, 4 * n:4 * n + 4], t_buf[:], vT_hi[:, 4 * n:4 * n + 4].bitcast(f32),
                                        ALU.subtract).then_inc(vlo_ready, 1)

            def out1_rows(n):
                dve.wait_ge(w_used[RING - 1], rounds(S_OUT1, 0, 0, 8 * n + 7))
                if n == 0:
                    dve.wait_ge(bcast1_in, 32)
                c = slice(n * NCOL, (n + 1) * NCOL)
                for m in range(MT):
                    last = nc.vector.tensor_tensor(y1[:, m, c], acc[:, n % 2, m], bout[:, c], ALU.add)
                last.then_inc(acc_read, 1)
                dve.wait_ge(acc_read, NG + n + 1)
                dve.sem_inc(y_ready, 1)
                for m in range(MT):
                    last = nc.vector.tensor_tensor(yg1[:, m, c], y1[:, m, c], gpost1[:, c], ALU.mult)
                last.then_inc(yg_ready, 1)

            for s in range(SLICES, 4 * SLICES):
                low(S_OUT1, 0, 0, s)
                if s % SLICES == 3:
                    out1_rows(s // SLICES - 1)
            out1_rows(NG - 1)
            dve.wait_ge(ssq_ready, 20)
            nc.vector.reduce_sum(mean_sum, ssq, AX.X).then_inc(sum_ready, 1)
            dve.wait_ge(sum_ready, 2)
            mean_square(mean_sum)
            dve.wait_ge(rms_ready, 4)
            dve.wait_ge(yg_ready, NG)
            for n in range(NG):
                residual(n, 3, yg1, o_ready)

        @block.gpsimd
        def _(pool):
            nc.gpsimd.memset(m_half, -0.5).then_inc(const_set, 1)
            pool.wait_ge(const_set, 1)

            def inverse_root(out_, in_, ready, count, done):
                pool.wait_ge(ready, count)
                nc.gpsimd.tensor_tensor(out_, in_, m_half, ALU.pow).then_inc(done, 1)

            inverse_root(rms[0], mean_sq, ms_ready, 1, rms_ready)
            pool.wait_ge(rope_in, 48)

            def rotate(row, block_no, steps):
                pool.wait_ge(rows_out, block_no)
                for m in range(MT):
                    v = row[:, m].rearrange("p (h d) -> p h d", h=G)
                    t = rope_t[:, m].rearrange("p (h d) -> p h d", h=G)
                    for a in range(2):
                        o = slice(a * HALF, (a + 1) * HALF)
                        w = slice((1 - a) * HALF, (2 - a) * HALF)
                        last = nc.gpsimd.tensor_tensor(
                            t[:, :, o], v[:, :, w], sin_t[:, m:m + 1, o].to_broadcast([P, G, HALF]), ALU.mult)
                last.then_inc(rope_step, 1)
                pool.wait_ge(rope_step, steps + 1)
                for m in range(MT):
                    v = row[:, m].rearrange("p (h d) -> p h d", h=G)
                    last = nc.gpsimd.tensor_tensor(v, v, cos_t[:, m:m + 1, :].to_broadcast([P, G, P]), ALU.mult)
                last.then_inc(rope_step, 1)
                pool.wait_ge(rope_step, steps + 2)
                last = nc.gpsimd.tensor_tensor(row[:], row[:], rope_t[:], ALU.add)
                last.then_inc(rope_step, 1)

            with pool.Fori(0, NG) as g:
                rotate(q_row, 4 * g + 1, 6 * g)
                rotate(k_row, 4 * g + 2, 6 * g + 3)

            def low(first, it, per, s):
                u = first // 2 + s // 2
                slot = s % RING
                half = s % 2
                pool.wait_ge(hi_ready[slot], rounds(first, it, per, s))
                nc.gpsimd.tensor_tensor(w_lo[:, slot], raw[:, u % LOADS, 2 * half:2 * half + 2], rd(w_hi, slot),
                                        ALU.subtract).then_inc(lo_ready[slot], 1)

            for s in range(RING):
                low(S_AG, 0, 16, s)
            inverse_root(rms[1], mean_sq, ms_ready, 2, rms_ready)
            for s in range(RING, 10):
                low(S_AG, 0, 16, s)
            inverse_root(rms[2], mean_sq, ms_ready, 3, rms_ready)
            for s in range(10, 2 * SLICES):
                low(S_AG, 0, 16, s)
            with pool.Fori(1, NG) as j:
                for s in range(2 * SLICES):
                    low(S_AG, j, 16, s)
            for s in range(4 * SLICES):
                low(S_Z, 0, 0, s)
                if s == 29:
                    inverse_root(rstd, var_eps, var_ready, 1, rstd_ready)
            for s in range(SLICES):
                low(S_OUT1, 0, 0, s)
            inverse_root(rms[3], mean_sq, ms_ready, 4, rms_ready)


_ROPE_THETA = 10000.0


def kernel(x, pre_norm_g, post_norm_g, attn_w_in, attn_w_out, conv_w_in, conv_b_in, conv_w_dw, conv_b_dw,
           conv_ln_g, conv_ln_b, conv_w_out, conv_b_out):
    import concourse.bacc as bacc
    from concourse.bass_utils import run_bass_kernel_spmd

    inv_freq = (1.0 / (_ROPE_THETA ** (np.arange(HALF, dtype=np.float32) * 2.0 / P))).astype(np.float32)
    ang = np.arange(SEQ, dtype=np.float32)[:, None] * inv_freq[None, :]
    cos, sin = np.cos(ang), np.sin(ang)
    by_row = lambda a: np.ascontiguousarray(a.reshape(MT, P, P).transpose(1, 0, 2), np.float32)
    ins = dict(
        x=x, pre_g=pre_norm_g, post_g=post_norm_g, w_in0=attn_w_in, w_out0=attn_w_out, w_in1=conv_w_in,
        b_in=conv_b_in, w_dw=conv_w_dw, b_dw=conv_b_dw, ln_g=conv_ln_g, ln_b=conv_ln_b, w_out1=conv_w_out,
        b_out=conv_b_out,
        rope_cos=by_row(np.concatenate([cos, cos], 1)), rope_sin=by_row(np.concatenate([-sin, sin], 1)),
        identity=np.eye(P, dtype=np.float32), causal=np.triu(np.full((P, P), -1e30, np.float32), 1))

    nc = bacc.Bacc("TRN2", target_bir_lowering=False, num_devices=1)
    arrays, args = {}, {}
    for name, value in ins.items():
        a = np.ascontiguousarray(value)
        arrays[f"in_{name}"] = a
        args[name] = nc.dram_tensor(f"in_{name}", a.shape, mybir.dt.from_np(a.dtype), kind="ExternalInput").ap()
    args["out"] = nc.dram_tensor("out", (1, SEQ, D), mybir.dt.float32, kind="ExternalOutput").ap()
    build(nc, **args)
    r = run_bass_kernel_spmd(nc, [arrays], core_ids=[0])
    return r.results[0]["out"]
```

```python
import numpy as np
from contextlib import ExitStack

import concourse.bass as bass
from concourse import mybir

P = 128
SEQ = 256
D = 2048
MT = SEQ // P
KT = D // P
NCOL = 512
SL_K = 2
SLICES = KT // SL_K
RING = 4
LOADS = 4
G = 4
NG = D // NCOL
HALF = 64
TAPS = 31
PAD = TAPS - 1
UW = PAD + SEQ
SCALE = float(P) ** -0.5
RMS_EPS = 1e-6
LN_EPS = 1e-5

S_QKVZ = 0
S_OUT0 = S_QKVZ + 4 * NG * SLICES
S_AG = S_OUT0 + NG * SLICES
S_Z = S_AG + 2 * NG * SLICES
S_OUT1 = S_Z + NG * SLICES

V_PRE0, V_PRE1, V_BA, V_BG, V_BDW, V_LNG, V_LNB = range(0, 7 * KT, KT)
NVEC = 7 * KT
FINAL_AT = (29, 31)
ROWS_AT = (7, 9, 11, 26)
DW_ROWS = TAPS * KT // 4


def build(nc, x, pre_g, post_g, w_in0, w_out0, w_in1, b_in, w_dw, b_dw, ln_g, ln_b, w_out1, b_out,
          rope_cos, rope_sin, identity, causal, out):
    f32, f32r = mybir.dt.float32, mybir.dt.float32r
    ALU, ACT, AX = mybir.AluOpType, mybir.ActivationFunctionType, mybir.AxisListType

    ctx = ExitStack()
    with ctx:
        def sem(name):
            return ctx.enter_context(nc.semaphore(name))

        arena = ctx.enter_context(nc.sbuf_tensor("arena", [P, 207 * 256], f32))
        KB = 1024
        base = nc.sbuf_base - 207 * KB

        def at(name, offset, shape, dt=f32):
            size = 4
            for n in shape[1:]:
                size *= n
            if dt == mybir.dt.bfloat16:
                size //= 2
            assert offset + size <= 207 * KB, name
            return nc.alloc_sbuf_tensor_at(name, shape, dt, offset=base + offset)

        raw = at("raw", 0, [P, LOADS, 4, NCOL])
        w_hi = at("w_hi", 32 * KB, [P, RING, SL_K, NCOL], f32r)
        w_lo = at("w_lo", 48 * KB, [P, RING, SL_K, NCOL], f32r)
        xrow = at("xrow", 64 * KB, [P, MT, D])
        A = 80 * KB
        xT_hi = at("xT_hi", A, [P, KT, SEQ], f32r)
        xT_lo = at("xT_lo", A + 16 * KB, [P, KT, SEQ], f32r)
        gpost0 = at("gpost0", A, [P, D])
        B = 112 * KB
        uT_hi = at("uT_hi", B, [P, KT, SEQ], f32r)
        uT_lo = at("uT_lo", B + 16 * KB, [P, KT, SEQ], f32r)
        c_row = at("c_row", B, [P, MT, D])
        z_row1 = at("z_row1", B + 16 * KB, [P, MT, D])
        y1 = at("y1", B, [P, MT, D])
        gpost1 = at("gpost1", B + 16 * KB, [P, D])
        bout = at("bout", B + 24 * KB, [P, D])
        Dr = 144 * KB
        q_row = at("q_row", Dr, [P, MT, NCOL])
        k_row = at("k_row", Dr + 4 * KB, [P, MT, NCOL])
        rope_t = at("rope_t", Dr + 8 * KB, [P, MT, NCOL])
        qT = at("qT", Dr + 12 * KB, [P, G, SEQ])
        kT = at("kT", Dr + 16 * KB, [P, G, SEQ])
        probs = at("probs", Dr + 20 * KB, [P, G, 3 * P])
        junk0 = at("junk0", Dr + 12 * KB, [P, D])
        y0 = at("y0", Dr, [P, MT, D])
        ag_row = at("ag_row", Dr, [P, 2, MT, NCOL])
        sig = at("sig", Dr + 8 * KB, [P, 2, 2, SEQ])
        u_pad = at("u_pad", Dr + 12 * KB, [P, KT, UW])
        junk2 = at("junk2", B, [P, D])
        yg1 = at("yg1", A, [P, MT, D])
        vT_hi = at("vT_hi", Dr, [P, KT, SEQ], f32r)
        vT_lo = at("vT_lo", Dr + 16 * KB, [P, KT, SEQ], f32r)
        C = 176 * KB
        v_row = at("v_row", C, [P, MT, NCOL])
        z_row = at("z_row", C + 4 * KB, [P, MT, NCOL])
        u_row = at("u_row", C + 8 * KB, [P, MT, NCOL])
        pT = at("pT", C + 12 * KB, [P, G, 3 * P])
        cT = at("cT", C, [P, KT, SEQ])
        junk1 = at("junk1", C + 16 * KB, [P, NCOL])
        t_buf = at("t_buf", C + 16 * KB, [P, G, SEQ])
        vec_rows = at("vec_rows", C, [NVEC, P])
        dw_rows = at("dw_rows", C + 512, [DW_ROWS, 4, P])
        vec = at("vec", C + 20 * KB, [P, NVEC])
        taps = at("taps", C + 20 * KB + 512, [P, TAPS * KT])
        cos_t = at("cos_t", C + 22 * KB + 512, [P, MT, P])
        sin_t = at("sin_t", C + 23 * KB + 512, [P, MT, P])
        ident = at("ident", C + 24 * KB + 512, [P, P])
        mask = at("mask", C + 25 * KB, [P, P])
        small = at("small", C + 25 * KB + 512, [P, 128])
        ident_b = at("ident_b", C + 26 * KB, [P, P], mybir.dt.bfloat16)
        mask_b = at("mask_b", C + 26 * KB + 256, [P, P], mybir.dt.bfloat16)
        ssq = small[:, 2:10].rearrange("p (m n) -> p m n", m=MT)
        mean_sq = small[:, 10:12]
        mean_sum = small[:, 0:2]
        rms = [small[:, 12 + 2 * i:14 + 2 * i] for i in range(4)]
        row_max = small[:, 20:28].rearrange("p (h m) -> p h m", h=G)
        neg_max = small[:, 28:36].rearrange("p (h m) -> p h m", h=G)
        row_sum = small[:, 36:44].rearrange("p (h m) -> p h m", h=G)
        inv_sum = small[:, 44:52].rearrange("p (h m) -> p h m", h=G)
        bn = small[:, 52:100].rearrange("p (m n s) -> p m n s", m=MT, n=NG)
        mv = small[:, 100:104].rearrange("p (m s) -> p m s", m=MT)
        rstd = small[:, 104:106]
        var_eps = small[:, 106:108]
        m_half = small[:, 108:110]

        acc = ctx.enter_context(nc.psum_tensor("acc", [P, 2, MT, NCOL], f32))
        X = [ctx.enter_context(nc.psum_tensor(f"X{i}", [P, NCOL], f32)) for i in range(4)]

        raw_ready = [sem(f"raw_ready{i}") for i in range(LOADS)]
        hi_ready = [sem(f"hi_ready{i}") for i in range(RING)]
        lo_ready = [sem(f"lo_ready{i}") for i in range(RING)]
        w_used = [sem(f"w_used{i}") for i in range(RING)]
        rows_out = sem("rows_out")
        acc_read = sem("acc_read")
        x_in = [sem(f"x_in{i}") for i in range(NG)]
        ident_in = sem("ident_in")
        vec_in = sem("vec_in")
        dw_in = sem("dw_in")
        rope_in = sem("rope_in")
        gpost0_in = sem("gpost0_in")
        bcast1_in = sem("bcast1_in")
        vec_T = sem("vec_T")
        vec_ready = sem("vec_ready")
        const_set = sem("const_set")
        xT_done = sem("xT_done")
        xhi_ready = sem("xhi_ready")
        xlo_ready = sem("xlo_ready")
        ssq_ready = sem("ssq_ready")
        ms_ready = sem("ms_ready")
        rms_ready = sem("rms_ready")
        rope_step = sem("rope_step")
        qT_done, kT_done = sem("qT_done"), sem("kT_done")
        qT_ready, kT_ready = sem("qT_ready"), sem("kT_ready")
        s_done = sem("s_done")
        max_ready = sem("max_ready")
        negmax_ready = sem("negmax_ready")
        p_ready = sem("p_ready")
        pT_done = sem("pT_done")
        pT_ready = sem("pT_ready")
        inv_ready = sem("inv_ready")
        pv_done = sem("pv_done")
        u_ready = sem("u_ready")
        uT_done = sem("uT_done")
        uhi_ready, ulo_ready = sem("uhi_ready"), sem("ulo_ready")
        sum_ready = sem("sum_ready")
        x1_ready = sem("x1_ready")
        agT_done = sem("agT_done")
        sig_ready = sem("sig_ready")
        pad_set = sem("pad_set")
        a_biased = sem("a_biased")
        gated = sem("gated")
        conv_step = sem("conv_step")
        conv_done = sem("conv_done")
        mask_ready = sem("mask_ready")
        cR_done = sem("cR_done")
        c_ready = sem("c_ready")
        bn_ready = sem("bn_ready")
        mv_ready = sem("mv_ready")
        var_ready = sem("var_ready")
        rstd_ready = sem("rstd_ready")
        norm_ready = sem("norm_ready")
        fT_done = sem("fT_done")
        silu_ready = sem("silu_ready")
        t_ready = sem("t_ready")
        vhi_ready, vlo_ready = sem("vhi_ready"), sem("vlo_ready")
        y_ready = sem("y_ready")
        yg_ready = sem("yg_ready")
        o_ready = sem("o_ready")
        stored = sem("stored")

        block = ctx.enter_context(nc.Block())

        def cols(w):
            return w.rearrange("(t p) n -> p t n", p=P)

        def rounds(first, it, per, s):
            return it * (per // RING) + (first + s) // RING + 1

        def loaded(first, it, per, s):
            n = it * (per // 2 // LOADS) + (first + s) // 2 // LOADS + 1
            if first == S_AG:
                return 16 * n + 16 * (n - S_AG // 2 // LOADS)
            return 16 * n + (16 * ((S_Z - S_AG) // 2 // LOADS) if first > S_AG else 0)

        def rd(t, slot):
            return t[:, slot].bitcast(f32)

        @block.sync
        def _(sp):
            def load(first, it, per, j, w, col):
                u = first // 2 + j
                slot = u % LOADS
                if first or not isinstance(it, int) or it or j >= LOADS:
                    for i in (0, 1):
                        sp.wait_ge(lo_ready[(2 * u + i) % RING],
                                   rounds(first - 2 * LOADS, it, per, 2 * j + i))
                kg = j % 4
                sp.dma_start(raw[:, slot], cols(w)[:, 4 * kg:4 * kg + 4, bass.ds(col, NCOL)]
                             ).then_inc(raw_ready[slot], 16)

            xv = x.rearrange("b (m p) n -> p (b m) n", p=P)
            sp.dma_start(ident[:], identity).then_inc(ident_in, 16)
            for n in range(NG):
                c = slice(n * NCOL, (n + 1) * NCOL)
                sp.dma_start(xrow[:, :, c], xv[:, :, c]).then_inc(x_in[n], 16)
                load(S_QKVZ, 0, 32, n, w_in0[0], 0)
            sp.dma_start(dw_rows[:], w_dw[0].rearrange("k (t c) -> (k t) c", c=P)
                         .rearrange("(q r) c -> r q c", r=DW_ROWS)).then_inc(dw_in, 16)

            for j in range(4, 16):
                load(S_QKVZ, 0, 32, j, w_in0[0], (j // 4) * D)
            with sp.Fori(1, NG) as g:
                for j in range(16):
                    load(S_QKVZ, g, 32, j, w_in0[0], g * NCOL + (j // 4) * D)
            for j in range(16):
                load(S_OUT0, 0, 32, j, w_out0[0], (j // 4) * NCOL)
                if j == 3:
                    sp.wait_ge(w_used[RING - 1], rounds(S_OUT0, 0, 0, -1))
                    sp.dma_start(gpost0[:], post_g[0:1].to_broadcast([P, D])).then_inc(gpost0_in, 16)
            with sp.Fori(0, NG) as i:
                for j in range(8):
                    u = S_AG // 2 + j
                    for r in (0, 1):
                        sp.wait_ge(lo_ready[(2 * u + r) % RING], rounds(S_AG - 2 * LOADS, i, 16, 2 * j + r))
                    kg = j % 4
                    for e in (0, 1):
                        sp.dma_start(raw[:, u % LOADS, :, e * SEQ:(e + 1) * SEQ],
                                     cols(w_in1[0])[:, 4 * kg:4 * kg + 4,
                                                    bass.ds(i * NCOL + (j // 4) * SEQ + e * D, SEQ)]
                                     ).then_inc(raw_ready[u % LOADS], 16)
            with sp.Fori(0, NG) as n:
                for j in range(4):
                    load(S_Z, n, 8, j, w_in1[0], n * NCOL + 2 * D)
            for j in range(16):
                load(S_OUT1, 0, 32, j, w_out1[0], (j // 4) * NCOL)
                if j == 5:
                    sp.wait_ge(fT_done, NG)
                    sp.dma_start(gpost1[:], post_g[1:2].to_broadcast([P, D])).then_inc(bcast1_in, 16)
                    sp.dma_start(bout[:], b_out[0:1].to_broadcast([P, D])).then_inc(bcast1_in, 16)
            ov = out.rearrange("b (m p) n -> p (b m) n", p=P)
            for n in range(NG):
                c = slice(n * NCOL, (n + 1) * NCOL)
                sp.wait_ge(o_ready, n + 1)
                sp.dma_start(ov[:, :, c], xrow[:, :, c]).then_inc(stored, 16)
            sp.wait_ge(stored, 16 * NG)

        @block.tensor
        def _(pe):
            def slice_products(first, it, per, s, hi, lo):
                slot = s % RING
                par = ((first + s) // SLICES) % 2
                pe.wait_ge(lo_ready[slot], rounds(first, it, per, s))
                for i in range(SL_K):
                    k = SL_K * (s % SLICES) + i
                    for m in range(MT):
                        rows = slice(m * P, (m + 1) * P)
                        a = acc[:, par, m]
                        nc.tensor.matmul(a, hi[:, k, rows], w_hi[:, slot, i], start=(k == 0), stop=False)
                        nc.tensor.matmul(a, hi[:, k, rows], w_lo[:, slot, i], start=False, stop=False)
                        last = nc.tensor.matmul(a, lo[:, k, rows], w_hi[:, slot, i], start=False,
                                                stop=(k == KT - 1))
                last.then_inc(w_used[slot], 1)

            def pair_T(rows, bank, tile):
                for i in range(2):
                    for m in range(MT):
                        last = nc.tensor.transpose(bank[:, i * SEQ + m * P:i * SEQ + (m + 1) * P],
                                                   rows[:, m, (tile + i) * P:(tile + i + 1) * P], ident[:])
                return last

            def acc_free(b):
                o = b - 2
                if 0 <= o < 32:
                    pe.wait_ge(rows_out, o + 1)
                if 16 <= o < 20:
                    pe.wait_ge(acc_read, o - 15)
                if o >= 32:
                    pe.wait_ge(acc_read, o - 27)

            def input_T(layer, h):
                if layer == 0:
                    if h % 2 == 0:
                        pe.wait_ge(x_in[h // 2], 16)
                    if h == 3:
                        pe.wait_ge(vec_ready, 1)
                else:
                    pe.wait_ge(x1_ready, h + 1)
                if h >= 4:
                    pe.wait_ge(xlo_ready, SLICES * layer + h - 3)
                pair_T(xrow, X[h % 4], 2 * h).then_inc(xT_done, 1)

            def first_block(layer, first, per):
                for h in range(SLICES):
                    pe.wait_ge(xlo_ready, SLICES * layer + h + 1)
                    slice_products(first, 0, per, h, xT_hi, xT_lo)
                    if h + 3 < SLICES:
                        input_T(layer, h + 3)

            pe.wait_ge(ident_in, 16)
            input_T(0, 0)
            pe.wait_ge(vec_in, 16 * 5)
            nc.tensor.transpose(X[3][:, 0:NVEC], vec_rows[:], ident[0:NVEC, 0:NVEC]).then_inc(vec_T, 1)
            input_T(0, 1)
            input_T(0, 2)
            first_block(0, S_QKVZ, 32)

            def scores(g, h):
                s = X[h]
                nc.tensor.matmul(s[:, 0:P], qT[:, h, 0:P], kT[:, h, 0:P], start=True, stop=False)
                nc.tensor.matmul(s[:, 0:P], ident_b[:], mask_b[:], start=False, stop=True)
                nc.tensor.matmul(s[:, P:2 * P], qT[:, h, P:SEQ], kT[:, h, 0:P], start=True, stop=True)
                nc.tensor.matmul(s[:, 2 * P:3 * P], qT[:, h, P:SEQ], kT[:, h, P:SEQ], start=True, stop=False)
                nc.tensor.matmul(s[:, 2 * P:3 * P], ident_b[:], mask_b[:], start=False, stop=True
                                 ).then_inc(s_done, 1)

            def probs_T(g, h):
                pe.wait_ge(p_ready, G * g + h + 1)
                for i in range(3):
                    last = nc.tensor.transpose(X[h][:, i * P:(i + 1) * P], probs[:, h, i * P:(i + 1) * P], ident[:])
                last.then_inc(pT_done, 1)

            def values(g):
                pe.wait_ge(pT_ready, G * (g + 1))
                pe.wait_ge(rows_out, 4 * g + 3)
                for h in range(G):
                    c = slice(h * P, (h + 1) * P)
                    nc.tensor.matmul(X[0][:, c], pT[:, h, 0:P], v_row[:, 0, c], start=True, stop=True)
                    nc.tensor.matmul(X[1][:, c], pT[:, h, P:2 * P], v_row[:, 0, c], start=True, stop=False)
                    last = nc.tensor.matmul(X[1][:, c], pT[:, h, 2 * P:3 * P], v_row[:, 1, c],
                                            start=False, stop=True)
                last.then_inc(pv_done, 1)

            def gated_T(g):
                pe.wait_ge(u_ready, g + 1)
                pair_T(u_row, X[2], 0)
                pair_T(u_row, X[3], 2).then_inc(uT_done, 1)

            def group(g, first):
                for s in range(SLICES if first else 0, 4 * SLICES):
                    if s % SLICES == 0 and not (first and s < 2 * SLICES):
                        pe.wait_ge(rows_out, 4 * g + s // SLICES - 1)
                    slice_products(S_QKVZ, g, 32, s, xT_hi, xT_lo)
                    if s == 3 and not first:
                        gated_T(g - 1)
                    if s == 9 and first:
                        pe.wait_ge(dw_in, 16)
                        for q in range(4):
                            last = nc.tensor.transpose(X[0][:, q * DW_ROWS:(q + 1) * DW_ROWS], dw_rows[:, q, :],
                                                       ident[0:DW_ROWS, 0:DW_ROWS])
                        last.then_inc(vec_T, 1)
                    if s == 14:
                        pe.wait_ge(rope_step, 6 * g + 3)
                        if first:
                            pe.wait_ge(vec_ready, 2)
                        else:
                            pe.wait_ge(u_ready, g)
                        pair_T(q_row, X[0], 0)
                        pair_T(q_row, X[1], 2).then_inc(qT_done, 1)
                    if s == 20:
                        pe.wait_ge(rope_step, 6 * g + 6)
                        if not first:
                            pe.wait_ge(ulo_ready, g)
                        pair_T(k_row, X[2], 0)
                        pair_T(k_row, X[3], 2).then_inc(kT_done, 1)
                    if s == 22:
                        if first:
                            pe.wait_ge(mask_ready, 2)
                        pe.wait_ge(qT_ready, g + 1)
                        pe.wait_ge(kT_ready, g + 1)
                        for h in range(G):
                            scores(g, h)
                    if s in (26, 27):
                        for h in (0, 1) if s == 26 else (2, 3):
                            probs_T(g, h)
                    if s == 30:
                        values(g)

            group(0, True)
            with pe.Fori(1, NG) as g:
                group(g, False)

            for s in range(4 * SLICES):
                if s % SLICES == 0:
                    acc_free(16 + s // SLICES)
                if s % 2 == 0 and s < SLICES:
                    pe.wait_ge(ulo_ready, s // 2 + 1)
                slice_products(S_OUT0, 0, 0, s, uT_hi, uT_lo)
                if s == 3:
                    gated_T(NG - 1)

            acc_free(20)
            pe.wait_ge(ulo_ready, NG)
            for h in range(3):
                input_T(1, h)
            first_block(1, S_AG, 16)

            def conv_input_pair(h, buf, first):
                pe.wait_ge(rows_out, 20 + h + 1)
                if not first:
                    pe.wait_ge(sig_ready, h)
                pair_T(ag_row[:, buf], X[0], 0)
                pair_T(ag_row[:, buf], X[1], 2).then_inc(agT_done, 1)

            def two_blocks(i, first):
                for s in range(SLICES if first else 0, 2 * SLICES):
                    if s % SLICES == 0:
                        if first:
                            acc_free(20 + s // SLICES)
                        else:
                            pe.wait_ge(rows_out, 20 + 2 * i + s // SLICES - 1)
                    slice_products(S_AG, i, 16, s, xT_hi, xT_lo)
                    if s == 1 and not first:
                        conv_input_pair(2 * i - 1, 1, False)
                    if s == 9:
                        conv_input_pair(2 * i, 0, first)

            two_blocks(0, True)
            with pe.Fori(1, NG) as i:
                two_blocks(i, False)

            def conv_rows(j):
                pe.wait_ge(conv_done, G * (j + 1))
                if j:
                    pe.wait_ge(c_ready, MT * j)
                else:
                    pe.wait_ge(sig_ready, 2 * NG)
                for m in range(MT):
                    for c in range(G):
                        last = nc.tensor.transpose(X[3 - 3 * m][:, c * P:(c + 1) * P],
                                                   cT[:, G * j + c, m * P:(m + 1) * P], ident[:])
                    last.then_inc(cR_done, 1)

            def final_T(n):
                pe.wait_ge(norm_ready, n + 1)
                pe.wait_ge(rows_out, 28 + n + 1)
                if n:
                    pe.wait_ge(silu_ready, n)
                    pe.wait_ge(t_ready, n)
                for b in range(2):
                    pair_T(c_row, X[b], 4 * n + 2 * b)
                    last = pair_T(z_row1, X[2 + b], 4 * n + 2 * b)
                last.then_inc(fT_done, 1)

            for s in range(4 * SLICES):
                if s % SLICES == 0:
                    acc_free(28 + s // SLICES)
                slice_products(S_Z, 0, 0, s, xT_hi, xT_lo)
                if s == 1:
                    conv_input_pair(2 * NG - 1, 1, False)
                if s in ROWS_AT:
                    conv_rows(ROWS_AT.index(s))
                if s in FINAL_AT:
                    final_T(FINAL_AT.index(s))

            for s in range(4 * SLICES):
                if s % SLICES == 0:
                    acc_free(32 + s // SLICES)
                if s < SLICES and s % 2 == 0:
                    pe.wait_ge(vlo_ready, s // 2 + 1)
                slice_products(S_OUT1, 0, 0, s, vT_hi, vT_lo)
                if s in (0, 2):
                    final_T(2 + s // 2)

        @block.scalar
        def _(act):
            def high(first, it, per, s):
                u = first // 2 + s // 2
                slot = s % RING
                act.wait_ge(raw_ready[u % LOADS], loaded(first, it, per, s))
                if first or not isinstance(it, int) or it or s >= RING:
                    act.wait_ge(w_used[slot], rounds(first - RING, it, per, s))
                half = s % 2
                nc.scalar.activation(w_hi[:, slot], raw[:, u % LOADS, 2 * half:2 * half + 2], ACT.Copy
                                     ).then_inc(hi_ready[slot], 1)

            def block_rows(first, it, per, s, dst, scale, func=ACT.Copy):
                act.wait_ge(w_used[RING - 1], rounds(first, it, per, s))
                par = ((first + s) // SLICES) % 2
                for m in range(MT):
                    last = nc.scalar.activation(dst[:, m], acc[:, par, m], func, scale=scale[:, m:m + 1])
                last.then_inc(rows_out, 1)

            def input_high(layer, n, vcol):
                act.wait_ge(xT_done, SLICES * layer + n + 1)
                for c in range(2):
                    t = 2 * n + c
                    last = nc.scalar.activation(
                        xT_hi[:, t], X[n % 4][:, c * SEQ:(c + 1) * SEQ], ACT.Copy,
                        scale=vec[:, vcol + t:vcol + t + 1])
                last.then_inc(xhi_ready, 1)

            def squares(junk, row, m, n, before):
                if before:
                    act.wait_ge(ssq_ready, before)
                nc.scalar.activation(junk, row, ACT.Square, accum_out=ssq[:, m, n:n + 1]).then_inc(ssq_ready, 1)

            for v, n, src in ((V_PRE0, 2 * KT, pre_g), (V_BA, 2 * KT, b_in), (V_BDW, KT, b_dw),
                              (V_LNG, KT, ln_g), (V_LNB, KT, ln_b)):
                act.dma_start(vec_rows[v:v + n, :], src.rearrange("l (t c) -> (l t) c", c=P)).then_inc(vec_in, 16)
            act.dma_start(cos_t[:], rope_cos).then_inc(rope_in, 16)
            act.dma_start(sin_t[:], rope_sin).then_inc(rope_in, 16)
            act.dma_start(mask[:], causal).then_inc(rope_in, 16)

            act.wait_ge(vec_T, 1)
            nc.scalar.activation(vec[:], X[3][:, 0:NVEC], ACT.Copy).then_inc(vec_ready, 1)
            act.wait_ge(vec_ready, 1)
            for h in range(SLICES):
                input_high(0, h, V_PRE0)
                high(S_QKVZ, 0, 32, h)
            for m in range(MT):
                squares(junk0[:], xrow[:, m], m, 0, m)

            def heads_high(g):
                act.wait_ge(uT_done, g + 1)
                for b in range(2):
                    last = nc.scalar.activation(uT_hi[:, bass.ds(g * 4 + 2 * b, 2)], X[2 + b][:], ACT.Copy)
                last.then_inc(uhi_ready, 1)

            def group_end(s, g):
                if s == 3:
                    if not (isinstance(g, int) and g == 0):
                        act.wait_ge(u_ready, g)
                    block_rows(S_QKVZ, g, 32, 31, z_row, rms[0], ACT.Silu)
                if s == 7:
                    heads_high(g)

            def exponentials(g, h, first):
                if h == 0 and not first:
                    act.wait_ge(pT_done, G * g)
                act.wait_ge(negmax_ready, G * g + h + 1)
                for m in range(MT):
                    c = slice(0, P) if m == 0 else slice(P, 3 * P)
                    last = nc.scalar.activation(probs[:, h, c], X[h][:, c], ACT.Exp, bias=neg_max[:, h, m:m + 1],
                                                scale=SCALE, accum_out=row_sum[:, h, m:m + 1])
                last.then_inc(p_ready, 1)

            def group(g, first):
                for s in range(SLICES if first else 0, 4 * SLICES):
                    high(S_QKVZ, g, 32, s)
                    if not first:
                        group_end(s, g - 1)
                    if s == 12 and first:
                        act.wait_ge(vec_T, 2)
                        nc.scalar.activation(taps[:], X[0][:, 0:TAPS * KT], ACT.Copy).then_inc(vec_ready, 1)
                    if s == 11:
                        if first:
                            act.wait_ge(rms_ready, 1)
                        block_rows(S_QKVZ, g, 32, 7, q_row, rms[0])
                    if s == 18:
                        act.wait_ge(qT_done, g + 1)
                        for b in range(2):
                            last = nc.scalar.activation(qT[:, 2 * b:2 * b + 2], X[b][:], ACT.Copy)
                        last.then_inc(qT_ready, 1)
                    if s == 19:
                        block_rows(S_QKVZ, g, 32, 15, k_row, rms[0])
                    if s == 24:
                        act.wait_ge(kT_done, g + 1)
                        for b in range(2):
                            last = nc.scalar.activation(kT[:, 2 * b:2 * b + 2], X[2 + b][:], ACT.Copy)
                        last.then_inc(kT_ready, 1)
                    if s == 27:
                        if not first:
                            act.wait_ge(pv_done, g)
                        block_rows(S_QKVZ, g, 32, 23, v_row, rms[0])
                    if s in (26, 27, 28, 29):
                        exponentials(g, s - 26, first)

            group(0, True)
            with act.Fori(1, NG) as g:
                group(g, False)

            def out0_squares(n):
                act.wait_ge(w_used[RING - 1], rounds(S_OUT0, 0, 0, 8 * n + 7))
                for m in range(MT):
                    squares(junk1[:], acc[:, n % 2, m], m, n, 2 + MT * n + m)
                act.wait_ge(ssq_ready, 2 + MT * (n + 1))
                act.sem_inc(rows_out, 1)

            for s in range(4 * SLICES):
                high(S_OUT0, 0, 0, s)
                group_end(s, NG - 1)
                if s % SLICES == 3 and s > SLICES:
                    out0_squares(s // SLICES - 1)
            for s in range(RING):
                high(S_AG, 0, 16, s)
            out0_squares(NG - 1)
            for h in range(SLICES):
                if h >= RING:
                    high(S_AG, 0, 16, h)
                input_high(1, h, V_PRE1)
            for m in range(MT):
                squares(junk2[:], xrow[:, m], m, 0, 10 + m)

            def conv_input_parts(h, buf, first):
                act.wait_ge(agT_done, h + 1)
                if not first:
                    act.wait_ge(gated, h - 1)
                for c in range(2):
                    last = nc.scalar.activation(u_pad[:, bass.ds(h * 2 + c, 1), PAD:UW],
                                                X[0][:, c * SEQ:(c + 1) * SEQ], ACT.Identity,
                                                bias=vec[:, bass.ds(h * 2 + V_BA + c, 1)])
                for c in range(2):
                    last = nc.scalar.activation(sig[:, buf, c], X[1][:, c * SEQ:(c + 1) * SEQ], ACT.Sigmoid,
                                                bias=vec[:, bass.ds(h * 2 + V_BG + c, 1)])
                last.then_inc(sig_ready, 1)

            def two_blocks(i, first):
                for s in range(SLICES if first else 0, 2 * SLICES):
                    high(S_AG, i, 16, s)
                    if s == 3 and not first:
                        block_rows(S_AG, i - 1, 16, 15, ag_row[:, 1], rms[2])
                    if s == 5 and not first:
                        conv_input_parts(2 * i - 1, 1, False)
                    if s == 11:
                        if first:
                            act.wait_ge(rms_ready, 3)
                        block_rows(S_AG, i, 16, 7, ag_row[:, 0], rms[2])
                    if s == 13:
                        if first:
                            act.wait_ge(pad_set, 1)
                        conv_input_parts(2 * i, 0, first)

            two_blocks(0, True)
            with act.Fori(1, NG) as i:
                two_blocks(i, False)

            for s in range(4 * SLICES):
                high(S_Z, 0, 0, s)
                if s == 3:
                    block_rows(S_AG, NG - 1, 16, 15, ag_row[:, 1], rms[2])
                if s == 5:
                    conv_input_parts(2 * NG - 1, 1, False)
                if s % SLICES == 3 and s > SLICES:
                    n = s // SLICES - 1
                    block_rows(S_Z, 0, 0, 8 * n + 7, z_row1[:, :, n * NCOL:(n + 1) * NCOL], rms[2], ACT.Silu)
                for j in range(NG):
                    for m in range(MT):
                        if s == ROWS_AT[j] + 3:
                            act.wait_ge(cR_done, MT * j + m + 1)
                            nc.scalar.activation(c_row[:, m, j * NCOL:(j + 1) * NCOL], X[3 - 3 * m][:], ACT.Copy
                                                 ).then_inc(c_ready, 1)

            def affine_silu(n):
                act.wait_ge(fT_done, n + 1)
                if n:
                    act.wait_ge(vlo_ready, n)
                for c in range(4):
                    t = 4 * n + c
                    last = nc.scalar.activation(t_buf[:, c], X[c // 2][:, (c % 2) * SEQ:(c % 2 + 1) * SEQ], ACT.Silu,
                                                scale=vec[:, V_LNG + t:V_LNG + t + 1],
                                                bias=vec[:, V_LNB + t:V_LNB + t + 1])
                last.then_inc(silu_ready, 1)

            def final_high(n):
                act.wait_ge(t_ready, n + 1)
                nc.scalar.activation(vT_hi[:, 4 * n:4 * n + 4], t_buf[:], ACT.Copy).then_inc(vhi_ready, 1)

            def out1_squares(n):
                act.wait_ge(y_ready, n + 1)
                for m in range(MT):
                    squares(junk1[:], y1[:, m, n * NCOL:(n + 1) * NCOL], m, n, 12 + MT * n + m)

            for s in range(4 * SLICES):
                high(S_OUT1, 0, 0, s)
                if s in (0, 2, 4, 6):
                    affine_silu(s // 2)
                if s in (1, 3, 5, 7):
                    final_high(s // 2)
                if s == 3:
                    block_rows(S_Z, 0, 0, 31, z_row1[:, :, 3 * NCOL:4 * NCOL], rms[2], ACT.Silu)
                if s % SLICES == 4 and s > SLICES:
                    out1_squares(s // SLICES - 1)
            out1_squares(NG - 1)

        @block.vector
        def _(dve):
            def low(first, it, per, s):
                u = first // 2 + s // 2
                slot = s % RING
                half = s % 2
                dve.wait_ge(hi_ready[slot], rounds(first, it, per, s))
                nc.vector.tensor_tensor(w_lo[:, slot], raw[:, u % LOADS, 2 * half:2 * half + 2], rd(w_hi, slot),
                                        ALU.subtract).then_inc(lo_ready[slot], 1)

            def input_low(layer, n, vcol):
                dve.wait_ge(xhi_ready, SLICES * layer + n + 1)
                for c in range(2):
                    t = 2 * n + c
                    last = nc.vector.scalar_tensor_tensor(
                        out=xT_lo[:, t], in0=X[n % 4][:, c * SEQ:(c + 1) * SEQ],
                        scalar=vec[:, vcol + t:vcol + t + 1], in1=xT_hi[:, t].bitcast(f32),
                        op0=ALU.mult, op1=ALU.subtract)
                last.then_inc(xlo_ready, 1)

            def mean_square(first):
                nc.vector.tensor_scalar(mean_sq, first, 1.0 / D, RMS_EPS, ALU.mult, ALU.add).then_inc(ms_ready, 1)

            for h in range(SLICES):
                input_low(0, h, V_PRE0)
                low(S_QKVZ, 0, 32, h)
            dve.wait_ge(rope_in, 48)
            dve.wait_ge(ident_in, 16)
            nc.vector.tensor_copy(ident_b[:], ident[:]).then_inc(mask_ready, 1)
            nc.vector.tensor_copy(mask_b[:], mask[:]).then_inc(mask_ready, 1)
            dve.wait_ge(ssq_ready, 2)
            mean_square(ssq[:, :, 0])

            def gate_outputs(g):
                dve.wait_ge(pv_done, g + 1)
                dve.wait_ge(rows_out, 4 * (g + 1))
                dve.wait_ge(inv_ready, g + 1)
                for m in range(MT):
                    for h in range(G):
                        c = slice(h * P, (h + 1) * P)
                        last = nc.vector.scalar_tensor_tensor(
                            out=u_row[:, m, c], in0=X[m][:, c], scalar=inv_sum[:, h, m:m + 1], in1=z_row[:, m, c],
                            op0=ALU.mult, op1=ALU.mult)
                last.then_inc(u_ready, 1)

            def heads_low(g):
                dve.wait_ge(uhi_ready, g + 1)
                for b in range(2):
                    t = bass.ds(g * 4 + 2 * b, 2)
                    last = nc.vector.tensor_tensor(uT_lo[:, t], X[2 + b][:].rearrange("p (t r) -> p t r", t=2),
                                                   uT_hi[:, t].bitcast(f32), ALU.subtract)
                last.then_inc(ulo_ready, 1)

            def group_end(s, g):
                if s == 4:
                    gate_outputs(g)
                if s == 7:
                    heads_low(g)

            def maxima(g, h):
                dve.wait_ge(s_done, G * g + h + 1)
                nc.vector.reduce_max(row_max[:, h, 0:1], X[h][:, 0:P], AX.X)
                nc.vector.reduce_max(row_max[:, h, 1:2], X[h][:, P:3 * P], AX.X).then_inc(max_ready, 1)
                dve.wait_ge(max_ready, G * g + h + 1)
                nc.vector.tensor_scalar(neg_max[:, h], row_max[:, h], -SCALE, None, ALU.mult
                                        ).then_inc(negmax_ready, 1)

            def group(g, first):
                for s in range(SLICES if first else 0, 4 * SLICES):
                    low(S_QKVZ, g, 32, s)
                    if not first:
                        group_end(s, g - 1)
                    if s in (26, 27):
                        for h in (0, 1) if s == 26 else (2, 3):
                            maxima(g, h)
                    if s in (30, 31):
                        for h in (0, 1) if s == 30 else (2, 3):
                            dve.wait_ge(pT_done, G * g + h + 1)
                            nc.vector.tensor_copy(pT[:, h], X[h][:, 0:3 * P]).then_inc(pT_ready, 1)
                    if s == 31:
                        dve.wait_ge(p_ready, G * g + 4)
                        nc.vector.reciprocal(small[:, 44:52], small[:, 36:44]).then_inc(inv_ready, 1)

            group(0, True)
            with dve.Fori(1, NG) as g:
                group(g, False)

            def out0_rows(n):
                if n == 0:
                    dve.wait_ge(gpost0_in, 16)
                for m in range(MT):
                    dve.wait_ge(ssq_ready, 2 + MT * n + m + 1)
                    c = slice(n * NCOL, (n + 1) * NCOL)
                    last = nc.vector.tensor_tensor(y0[:, m, c], acc[:, n % 2, m], gpost0[:, c], ALU.mult)
                last.then_inc(acc_read, 1)

            for s in range(4 * SLICES):
                low(S_OUT0, 0, 0, s)
                group_end(s, NG - 1)
                if s % SLICES == 3 and s > SLICES:
                    out0_rows(s // SLICES - 1)
            out0_rows(NG - 1)

            def residual(h, w, r, y, done):
                for m in range(MT):
                    c = slice(h * w, (h + 1) * w)
                    last = nc.vector.scalar_tensor_tensor(
                        out=xrow[:, m, c], in0=y[:, m, c], scalar=rms[r][:, m:m + 1], in1=xrow[:, m, c],
                        op0=ALU.mult, op1=ALU.add)
                last.then_inc(done, 1)

            dve.wait_ge(ssq_ready, 10)
            nc.vector.reduce_sum(mean_sum, ssq, AX.X).then_inc(sum_ready, 1)
            dve.wait_ge(sum_ready, 1)
            mean_square(mean_sum)
            dve.wait_ge(rms_ready, 2)
            dve.wait_ge(acc_read, NG)
            residual(0, SEQ, 1, y0, x1_ready)
            for h in range(SLICES):
                if h + 1 < SLICES:
                    residual(h + 1, SEQ, 1, y0, x1_ready)
                input_low(1, h, V_PRE1)
            dve.wait_ge(x1_ready, SLICES)
            nc.vector.memset(u_pad[:, :, 0:PAD], 0.0).then_inc(pad_set, 1)
            dve.wait_ge(ssq_ready, 12)
            mean_square(ssq[:, :, 0])
            dve.wait_ge(pad_set, 1)

            def conv_tap(tile, c, k, steps):
                part = X[2][:, c * SEQ:(c + 1) * SEQ]
                last = k == TAPS - 1
                u = u_pad[:, bass.ds(tile, 1), k:k + SEQ]
                out_ = cT[:, bass.ds(tile, 1)] if last else part
                if k == 0:
                    ins = nc.vector.tensor_scalar(part, u, taps[:, bass.ds(tile, 1)],
                                                  vec[:, bass.ds(tile + V_BDW, 1)], ALU.mult, ALU.add)
                else:
                    dve.wait_ge(conv_step, steps)
                    ins = nc.vector.scalar_tensor_tensor(
                        out=out_, in0=u, scalar=taps[:, bass.ds(tile + k * KT, 1)], in1=part,
                        op0=ALU.mult, op1=ALU.add)
                ins.then_inc(conv_done if last else conv_step, 1)

            per_pair = 2 * (TAPS - 1)
            with dve.Fori(0, SLICES) as h:
                dve.wait_ge(sig_ready, h + 1)
                pair = u_pad[:, bass.ds(h * 2, 2), PAD:UW]
                for buf in range(1):
                    nc.vector.tensor_tensor(pair, pair, sig[:, bass.ds(h % 2, 1)].rearrange(
                        "p b c r -> p (b c) r"), ALU.mult).then_inc(gated, 1)
                dve.wait_ge(gated, h + 1)
                for k in range(TAPS):
                    for c in range(2):
                        conv_tap(h * 2 + c, c, k, h * per_pair + 2 * k - 1 + c)

            for n in range(NG):
                for m in range(MT):
                    dve.wait_ge(c_ready, MT * n + m + 1)
                    nc.vector.bn_stats(bn[:, m, n], c_row[:, m, n * NCOL:(n + 1) * NCOL]).then_inc(bn_ready, 1)
            dve.wait_ge(bn_ready, MT * NG)
            for m in range(MT):
                nc.vector.bn_aggr(mv[:, m], bn[:, m]).then_inc(mv_ready, 1)
            dve.wait_ge(mv_ready, MT)
            nc.vector.tensor_scalar(var_eps, mv[:, :, 1], LN_EPS, None, ALU.add).then_inc(var_ready, 1)
            dve.wait_ge(rstd_ready, 1)
            for n in range(NG):
                for m in range(MT):
                    c = c_row[:, m, n * NCOL:(n + 1) * NCOL]
                    last = nc.vector.tensor_scalar(c, c, mv[:, m, 0:1], rstd[:, m:m + 1], ALU.subtract, ALU.mult)
                last.then_inc(norm_ready, 1)

            for n in range(NG):
                dve.wait_ge(silu_ready, n + 1)
                for b in range(2):
                    part = t_buf[:, 2 * b:2 * b + 2]
                    last = nc.vector.tensor_tensor(part, part, X[2 + b][:].rearrange("p (t r) -> p t r", t=2), ALU.mult)
                last.then_inc(t_ready, 1)
                dve.wait_ge(vhi_ready, n + 1)
                nc.vector.tensor_tensor(vT_lo[:, 4 * n:4 * n + 4], t_buf[:], vT_hi[:, 4 * n:4 * n + 4].bitcast(f32),
                                        ALU.subtract).then_inc(vlo_ready, 1)

            def out1_rows(n):
                dve.wait_ge(w_used[RING - 1], rounds(S_OUT1, 0, 0, 8 * n + 7))
                if n == 0:
                    dve.wait_ge(bcast1_in, 32)
                c = slice(n * NCOL, (n + 1) * NCOL)
                for m in range(MT):
                    last = nc.vector.tensor_tensor(y1[:, m, c], acc[:, n % 2, m], bout[:, c], ALU.add)
                last.then_inc(acc_read, 1)
                dve.wait_ge(acc_read, NG + n + 1)
                dve.sem_inc(y_ready, 1)
                for m in range(MT):
                    last = nc.vector.tensor_tensor(yg1[:, m, c], y1[:, m, c], gpost1[:, c], ALU.mult)
                last.then_inc(yg_ready, 1)

            for s in range(SLICES, 4 * SLICES):
                low(S_OUT1, 0, 0, s)
                if s % SLICES == 3:
                    out1_rows(s // SLICES - 1)
            out1_rows(NG - 1)
            dve.wait_ge(ssq_ready, 20)
            nc.vector.reduce_sum(mean_sum, ssq, AX.X).then_inc(sum_ready, 1)
            dve.wait_ge(sum_ready, 2)
            mean_square(mean_sum)
            dve.wait_ge(rms_ready, 4)
            dve.wait_ge(yg_ready, NG)
            for n in range(NG):
                residual(n, NCOL, 3, yg1, o_ready)

        @block.gpsimd
        def _(pool):
            nc.gpsimd.memset(m_half, -0.5).then_inc(const_set, 1)
            pool.wait_ge(const_set, 1)

            def inverse_root(out_, in_, ready, count, done):
                pool.wait_ge(ready, count)
                nc.gpsimd.tensor_tensor(out_, in_, m_half, ALU.pow).then_inc(done, 1)

            inverse_root(rms[0], mean_sq, ms_ready, 1, rms_ready)
            pool.wait_ge(rope_in, 48)

            def rotate(row, block_no, steps):
                pool.wait_ge(rows_out, block_no)
                for m in range(MT):
                    v = row[:, m].rearrange("p (h d) -> p h d", h=G)
                    t = rope_t[:, m].rearrange("p (h d) -> p h d", h=G)
                    for a in range(2):
                        o = slice(a * HALF, (a + 1) * HALF)
                        w = slice((1 - a) * HALF, (2 - a) * HALF)
                        last = nc.gpsimd.tensor_tensor(
                            t[:, :, o], v[:, :, w], sin_t[:, m:m + 1, o].to_broadcast([P, G, HALF]), ALU.mult)
                last.then_inc(rope_step, 1)
                pool.wait_ge(rope_step, steps + 1)
                for m in range(MT):
                    v = row[:, m].rearrange("p (h d) -> p h d", h=G)
                    last = nc.gpsimd.tensor_tensor(v, v, cos_t[:, m:m + 1, :].to_broadcast([P, G, P]), ALU.mult)
                last.then_inc(rope_step, 1)
                pool.wait_ge(rope_step, steps + 2)
                last = nc.gpsimd.tensor_tensor(row[:], row[:], rope_t[:], ALU.add)
                last.then_inc(rope_step, 1)

            with pool.Fori(0, NG) as g:
                rotate(q_row, 4 * g + 1, 6 * g)
                rotate(k_row, 4 * g + 2, 6 * g + 3)

            def low(first, it, per, s):
                u = first // 2 + s // 2
                slot = s % RING
                half = s % 2
                pool.wait_ge(hi_ready[slot], rounds(first, it, per, s))
                nc.gpsimd.tensor_tensor(w_lo[:, slot], raw[:, u % LOADS, 2 * half:2 * half + 2], rd(w_hi, slot),
                                        ALU.subtract).then_inc(lo_ready[slot], 1)

            for s in range(RING):
                low(S_AG, 0, 16, s)
            inverse_root(rms[1], mean_sq, ms_ready, 2, rms_ready)
            for s in range(RING, 10):
                low(S_AG, 0, 16, s)
            inverse_root(rms[2], mean_sq, ms_ready, 3, rms_ready)
            for s in range(10, 2 * SLICES):
                low(S_AG, 0, 16, s)
            with pool.Fori(1, NG) as j:
                for s in range(2 * SLICES):
                    low(S_AG, j, 16, s)
            for s in range(4 * SLICES):
                low(S_Z, 0, 0, s)
            inverse_root(rstd, var_eps, var_ready, 1, rstd_ready)
            for s in range(SLICES):
                low(S_OUT1, 0, 0, s)
            inverse_root(rms[3], mean_sq, ms_ready, 4, rms_ready)


_ROPE_THETA = 10000.0


def kernel(x, pre_norm_g, post_norm_g, attn_w_in, attn_w_out, conv_w_in, conv_b_in, conv_w_dw, conv_b_dw,
           conv_ln_g, conv_ln_b, conv_w_out, conv_b_out):
    import concourse.bacc as bacc
    from concourse.bass_utils import run_bass_kernel_spmd

    inv_freq = (1.0 / (_ROPE_THETA ** (np.arange(HALF, dtype=np.float32) * 2.0 / P))).astype(np.float32)
    ang = np.arange(SEQ, dtype=np.float32)[:, None] * inv_freq[None, :]
    cos, sin = np.cos(ang), np.sin(ang)
    by_row = lambda a: np.ascontiguousarray(a.reshape(MT, P, P).transpose(1, 0, 2), np.float32)
    ins = dict(
        x=x, pre_g=pre_norm_g, post_g=post_norm_g, w_in0=attn_w_in, w_out0=attn_w_out, w_in1=conv_w_in,
        b_in=conv_b_in, w_dw=conv_w_dw, b_dw=conv_b_dw, ln_g=conv_ln_g, ln_b=conv_ln_b, w_out1=conv_w_out,
        b_out=conv_b_out,
        rope_cos=by_row(np.concatenate([cos, cos], 1)), rope_sin=by_row(np.concatenate([-sin, sin], 1)),
        identity=np.eye(P, dtype=np.float32), causal=np.triu(np.full((P, P), -1e30, np.float32), 1))

    nc = bacc.Bacc("TRN2", target_bir_lowering=False, num_devices=1)
    arrays, args = {}, {}
    for name, value in ins.items():
        a = np.ascontiguousarray(value)
        arrays[f"in_{name}"] = a
        args[name] = nc.dram_tensor(f"in_{name}", a.shape, mybir.dt.from_np(a.dtype), kind="ExternalInput").ap()
    args["out"] = nc.dram_tensor("out", (1, SEQ, D), mybir.dt.float32, kind="ExternalOutput").ap()
    build(nc, **args)
    r = run_bass_kernel_spmd(nc, [arrays], core_ids=[0])
    return r.results[0]["out"]
```

```python
import numpy as np
from contextlib import ExitStack

import concourse.bass as bass
from concourse import mybir

P = 128
SEQ = 256
D = 2048
MT = SEQ // P
KT = D // P
NCOL = 512
SL_K = 2
SLICES = KT // SL_K
RING = 4
LOADS = 4
G = 4
NG = D // NCOL
HALF = 64
TAPS = 31
PAD = TAPS - 1
UW = PAD + SEQ
SCALE = float(P) ** -0.5
RMS_EPS = 1e-6
LN_EPS = 1e-5

S_QKVZ = 0
S_OUT0 = S_QKVZ + 4 * NG * SLICES
S_AG = S_OUT0 + NG * SLICES
S_Z = S_AG + 2 * NG * SLICES
S_OUT1 = S_Z + NG * SLICES

V_PRE0, V_PRE1, V_BA, V_BG, V_BDW, V_LNG, V_LNB = range(0, 7 * KT, KT)
NPRE = 2 * KT
NVEC = 5 * KT
ROOT_AT = 30
FINAL_AT = (28, 30)
ROWS_AT = (7, 9, 11, 26)
LEAD = 2
SPLIT_AFTER = ((0,), (1,), (2,), (3,), (4, 5), (6,), (7, 8), (9,))
SQUARES_AFTER = (1, 2, 3, 5)
STAGED = (4, 1)
OUT_PARTS = [slice(0, 128), slice(128, 384), slice(384, 768), slice(768, 1088), slice(1088, 1408)]
POOL_COLS = slice(OUT_PARTS[-1].stop, D)
DW_ROWS = TAPS * KT // 4


def build(nc, x, pre_g, post_g, w_in0, w_out0, w_in1, b_in, w_dw, b_dw, ln_g, ln_b, w_out1, b_out,
          rope_cos, rope_sin, identity, causal, out):
    f32, f32r = mybir.dt.float32, mybir.dt.float32r
    ALU, ACT, AX = mybir.AluOpType, mybir.ActivationFunctionType, mybir.AxisListType

    ctx = ExitStack()
    with ctx:
        def sem(name):
            return ctx.enter_context(nc.semaphore(name))

        arena = ctx.enter_context(nc.sbuf_tensor("arena", [P, 207 * 256], f32))
        KB = 1024
        base = nc.sbuf_base - 207 * KB

        def at(name, offset, shape, dt=f32):
            size = 4
            for n in shape[1:]:
                size *= n
            if dt == mybir.dt.bfloat16:
                size //= 2
            assert offset + size <= 207 * KB, name
            return nc.alloc_sbuf_tensor_at(name, shape, dt, offset=base + offset)

        raw = at("raw", 0, [P, LOADS, 4, NCOL])
        w_hi = at("w_hi", 32 * KB, [P, RING, SL_K, NCOL], f32r)
        w_lo = at("w_lo", 48 * KB, [P, RING, SL_K, NCOL], f32r)
        xrow = at("xrow", 64 * KB, [P, MT, D])
        A = 80 * KB
        xT_hi = at("xT_hi", A, [P, KT, SEQ], f32r)
        xT_lo = at("xT_lo", A + 16 * KB, [P, KT, SEQ], f32r)
        gpost0 = at("gpost0", A, [P, D])
        B = 112 * KB
        uT_hi = at("uT_hi", B, [P, KT, SEQ], f32r)
        uT_lo = at("uT_lo", B + 16 * KB, [P, KT, SEQ], f32r)
        c_row = at("c_row", B, [P, MT, D])
        z_row1 = at("z_row1", B + 16 * KB, [P, MT, D])
        y1 = at("y1", B, [P, MT, D])
        gpost1 = at("gpost1", B + 16 * KB, [P, D])
        bout = at("bout", B + 24 * KB, [P, D])
        Dr = 144 * KB
        q_row = at("q_row", Dr, [P, MT, NCOL])
        k_row = at("k_row", Dr + 4 * KB, [P, MT, NCOL])
        rope_t = at("rope_t", Dr + 8 * KB, [P, MT, NCOL])
        qT = at("qT", Dr + 12 * KB, [P, G, SEQ])
        kT = at("kT", Dr + 16 * KB, [P, G, SEQ])
        probs = at("probs", Dr + 20 * KB, [P, G, 3 * P])
        junk0 = at("junk0", Dr + 12 * KB, [P, NCOL])
        y0 = at("y0", Dr, [P, MT, D])
        ag_row = at("ag_row", Dr, [P, 2, MT, NCOL])
        sig = at("sig", Dr + 8 * KB, [P, 2, 2, SEQ])
        u_pad = at("u_pad", Dr + 12 * KB, [P, KT, UW])
        junk2 = at("junk2", B, [P, NCOL])
        yg1 = at("yg1", A, [P, MT, D])
        vT_hi = at("vT_hi", Dr, [P, KT, SEQ], f32r)
        vT_lo = at("vT_lo", Dr + 16 * KB, [P, KT, SEQ], f32r)
        C = 176 * KB
        v_row = at("v_row", C, [P, MT, NCOL])
        z_row = at("z_row", C + 4 * KB, [P, MT, NCOL])
        u_row = at("u_row", C + 8 * KB, [P, MT, NCOL])
        pT = at("pT", C + 12 * KB, [P, G, 3 * P])
        cT = at("cT", C, [P, KT, SEQ])
        junk1 = at("junk1", C + 16 * KB, [P, NCOL])
        t_buf = at("t_buf", C + 16 * KB, [P, G, SEQ])
        vec_rows = at("vec_rows", C, [NVEC, P])
        dw_rows = at("dw_rows", C + 512, [DW_ROWS, 4, P])
        pre_rows = at("pre_rows", C + 2 * KB + 512, [NPRE, P])
        vec = at("vec", C + 20 * KB, [P, NPRE + NVEC])
        taps = at("taps", C + 20 * KB + 512, [P, TAPS * KT])
        cos_t = at("cos_t", C + 22 * KB + 512, [P, MT, P])
        sin_t = at("sin_t", C + 23 * KB + 512, [P, MT, P])
        ident = at("ident", C + 24 * KB + 512, [P, P])
        mask = at("mask", C + 25 * KB, [P, P])
        small = at("small", C + 25 * KB + 512, [P, 128])
        ident_b = at("ident_b", C + 26 * KB, [P, P], mybir.dt.bfloat16)
        mask_b = at("mask_b", C + 26 * KB + 256, [P, P], mybir.dt.bfloat16)
        idle = at("idle", C + 26 * KB + 512, [P, NCOL], mybir.dt.bfloat16)
        ssq = small[:, 2:10].rearrange("p (m n) -> p m n", m=MT)
        mean_sq = small[:, 10:12]
        mean_sum = small[:, 0:2]
        mean_part = small[:, 110:112]
        rms = [small[:, 12 + 2 * i:14 + 2 * i] for i in range(4)]
        row_max = small[:, 20:28].rearrange("p (h m) -> p h m", h=G)
        neg_max = small[:, 28:36].rearrange("p (h m) -> p h m", h=G)
        row_sum = small[:, 36:44].rearrange("p (h m) -> p h m", h=G)
        inv_sum = small[:, 44:52].rearrange("p (h m) -> p h m", h=G)
        bn = small[:, 52:100].rearrange("p (m n s) -> p m n s", m=MT, n=NG)
        mv = small[:, 100:104].rearrange("p (m s) -> p m s", m=MT)
        rstd = small[:, 104:106]
        var_eps = small[:, 106:108]
        m_half = small[:, 108:110]

        acc = ctx.enter_context(nc.psum_tensor("acc", [P, 2, MT, NCOL], f32))
        X = [ctx.enter_context(nc.psum_tensor(f"X{i}", [P, NCOL], f32)) for i in range(4)]

        raw_ready = [sem(f"raw_ready{i}") for i in range(LOADS)]
        hi_ready = [sem(f"hi_ready{i}") for i in range(RING)]
        lo_ready = [sem(f"lo_ready{i}") for i in range(RING)]
        w_used = [sem(f"w_used{i}") for i in range(RING)]
        rows_out = sem("rows_out")
        acc_read = sem("acc_read")
        half_in = [sem("half_in0"), sem("half_in1")]
        x0_in = sem("x0_in")
        x_in = [sem(f"x_in{i}") for i in range(NG)]
        ident_in = sem("ident_in")
        pre_in = sem("pre_in")
        vec_in = sem("vec_in")
        dw_in = sem("dw_in")
        rope_in = sem("rope_in")
        gpost0_in = sem("gpost0_in")
        bcast1_in = sem("bcast1_in")
        vec_T = sem("vec_T")
        vec_ready = sem("vec_ready")
        const_set = sem("const_set")
        xT_done = sem("xT_done")
        xhi_ready = sem("xhi_ready")
        xlo_ready = sem("xlo_ready")
        ssq_ready = sem("ssq_ready")
        ms_ready = sem("ms_ready")
        rms_ready = sem("rms_ready")
        rope_step = sem("rope_step")
        qT_done, kT_done = sem("qT_done"), sem("kT_done")
        qT_ready, kT_ready = sem("qT_ready"), sem("kT_ready")
        s_done = sem("s_done")
        max_ready = sem("max_ready")
        negmax_ready = sem("negmax_ready")
        p_ready = sem("p_ready")
        pT_done = sem("pT_done")
        pT_ready = sem("pT_ready")
        inv_ready = sem("inv_ready")
        pv_done = sem("pv_done")
        u_ready = sem("u_ready")
        uT_done = sem("uT_done")
        uhi_ready, ulo_ready = sem("uhi_ready"), sem("ulo_ready")
        sum_ready = sem("sum_ready")
        x1_ready = sem("x1_ready")
        agT_done = sem("agT_done")
        sig_ready = sem("sig_ready")
        pad_set = sem("pad_set")
        gated = sem("gated")
        conv_step = sem("conv_step")
        conv_done = sem("conv_done")
        mask_ready = sem("mask_ready")
        cR_done = sem("cR_done")
        c_ready = sem("c_ready")
        bn_ready = sem("bn_ready")
        mv_ready = sem("mv_ready")
        var_ready = sem("var_ready")
        rstd_ready = sem("rstd_ready")
        norm_ready = sem("norm_ready")
        fT_done = sem("fT_done")
        silu_ready = sem("silu_ready")
        t_ready = sem("t_ready")
        vhi_ready, vlo_ready = sem("vhi_ready"), sem("vlo_ready")
        y_ready = sem("y_ready")
        yg_ready = sem("yg_ready")
        o_ready = sem("o_ready")
        row0_done = sem("row0_done")
        part_ready = sem("part_ready")
        scaled = sem("scaled")
        o_pool = sem("o_pool")
        stored = sem("stored")

        block = ctx.enter_context(nc.Block())

        def cols(w):
            return w.rearrange("(t p) n -> p t n", p=P)

        def rounds(first, it, per, s):
            return it * (per // RING) + (first + s) // RING + 1

        def loaded(first, it, per, s):
            n = it * (per // 2 // LOADS) + (first + s) // 2 // LOADS + 1
            if first == S_AG:
                return 16 * n + 16 * (n - S_AG // 2 // LOADS)
            return 16 * n + (16 * ((S_Z - S_AG) // 2 // LOADS) if first > S_AG else 0)

        def rd(t, slot):
            return t[:, slot].bitcast(f32)

        @block.sync
        def _(sp):
            def load(first, it, per, j, w, col):
                u = first // 2 + j
                slot = u % LOADS
                if first or not isinstance(it, int) or it or j >= LOADS:
                    for i in (0, 1):
                        sp.wait_ge(lo_ready[(2 * u + i) % RING],
                                   rounds(first - 2 * LOADS, it, per, 2 * j + i))
                kg = j % 4
                sp.dma_start(raw[:, slot], cols(w)[:, 4 * kg:4 * kg + 4, bass.ds(col, NCOL)]
                             ).then_inc(raw_ready[slot], 16)

            xv = x.rearrange("b (m p) n -> p (b m) n", p=P)
            c = slice(0, SEQ)
            sp.dma_start(xrow[:, :, c], xv[:, :, c]).then_inc(x0_in, 16)
            sp.dma_start(ident[:], identity).then_inc(ident_in, 16)
            wv = cols(w_in0[0])

            def half_load(n, half, done):
                k = 2 * SL_K * n + SL_K * half
                sp.dma_start(raw[:, n, half * SL_K:(half + 1) * SL_K], wv[:, k:k + SL_K, 0:NCOL]).then_inc(done, 16)

            half_load(0, 0, half_in[0])
            c = slice(SEQ, NCOL)
            sp.dma_start(xrow[:, :, c], xv[:, :, c]).then_inc(x_in[0], 16)
            half_load(0, 1, raw_ready[0])
            for n in range(1, NG):
                c = slice(n * NCOL, (n + 1) * NCOL)
                sp.dma_start(xrow[:, :, c], xv[:, :, c]).then_inc(x_in[n], 16)
                if n == 1:
                    half_load(1, 0, half_in[1])
                    half_load(1, 1, raw_ready[1])
                else:
                    load(S_QKVZ, 0, 32, n, w_in0[0], 0)
            for v, rows, src in ((V_BA, 2 * KT, b_in), (V_BDW, KT, b_dw), (V_LNG, KT, ln_g), (V_LNB, KT, ln_b)):
                sp.dma_start(vec_rows[v - NPRE:v - NPRE + rows, :], src.rearrange("l (t c) -> (l t) c", c=P)
                             ).then_inc(vec_in, 16)
            sp.dma_start(cos_t[:], rope_cos).then_inc(rope_in, 16)
            sp.dma_start(sin_t[:], rope_sin).then_inc(rope_in, 16)
            sp.dma_start(mask[:], causal).then_inc(rope_in, 16)
            sp.dma_start(dw_rows[:], w_dw[0].rearrange("k (t c) -> (k t) c", c=P)
                         .rearrange("(q r) c -> r q c", r=DW_ROWS)).then_inc(dw_in, 16)

            for j in range(4, 16):
                load(S_QKVZ, 0, 32, j, w_in0[0], (j // 4) * D)
            with sp.Fori(1, NG) as g:
                for j in range(16):
                    load(S_QKVZ, g, 32, j, w_in0[0], g * NCOL + (j // 4) * D)
            for j in range(16):
                load(S_OUT0, 0, 32, j, w_out0[0], (j // 4) * NCOL)
                if j == 3:
                    sp.wait_ge(w_used[RING - 1], rounds(S_OUT0, 0, 0, -1))
                    sp.dma_start(gpost0[:], post_g[0:1].to_broadcast([P, D])).then_inc(gpost0_in, 16)
            with sp.Fori(0, NG) as i:
                for j in range(8):
                    u = S_AG // 2 + j
                    for r in (0, 1):
                        sp.wait_ge(lo_ready[(2 * u + r) % RING], rounds(S_AG - 2 * LOADS, i, 16, 2 * j + r))
                    kg = j % 4
                    for e in (0, 1):
                        sp.dma_start(raw[:, u % LOADS, :, e * SEQ:(e + 1) * SEQ],
                                     cols(w_in1[0])[:, 4 * kg:4 * kg + 4,
                                                    bass.ds(i * NCOL + (j // 4) * SEQ + e * D, SEQ)]
                                     ).then_inc(raw_ready[u % LOADS], 16)
            with sp.Fori(0, NG) as n:
                for j in range(4):
                    load(S_Z, n, 8, j, w_in1[0], n * NCOL + 2 * D)
            for j in range(16):
                load(S_OUT1, 0, 32, j, w_out1[0], (j // 4) * NCOL)
                if j == 5:
                    sp.wait_ge(fT_done, NG)
                    sp.dma_start(gpost1[:], post_g[1:2].to_broadcast([P, D])).then_inc(bcast1_in, 16)
                    sp.dma_start(bout[:], b_out[0:1].to_broadcast([P, D])).then_inc(bcast1_in, 16)
            ov = out.rearrange("b (m p) n -> p (b m) n", p=P)
            for n, c in enumerate(OUT_PARTS):
                sp.wait_ge(o_ready, n + 1)
                sp.dma_start(ov[:, :, c], xrow[:, :, c]).then_inc(stored, 16)
                if n in (2, 3):
                    sp.wait_ge(o_pool, n - 1)
                    sp.dma_start(ov[:, n - 2, POOL_COLS], xrow[:, n - 2, POOL_COLS]).then_inc(stored, 16)
            sp.wait_ge(stored, 16 * (len(OUT_PARTS) + MT))

        @block.tensor
        def _(pe):
            def slice_products(first, it, per, s, hi, lo, by_row=False):
                slot = s % RING
                par = ((first + s) // SLICES) % 2
                pe.wait_ge(lo_ready[slot], rounds(first, it, per, s))
                order = [(i, m) for i in range(SL_K) for m in range(MT)]
                if by_row:
                    order.sort(key=lambda im: im[1])
                for n, (i, m) in enumerate(order):
                    k = SL_K * (s % SLICES) + i
                    rows = slice(m * P, (m + 1) * P)
                    a = acc[:, par, m]
                    nc.tensor.matmul(a, hi[:, k, rows], w_hi[:, slot, i], start=(k == 0), stop=False)
                    nc.tensor.matmul(a, hi[:, k, rows], w_lo[:, slot, i], start=False, stop=False)
                    last = nc.tensor.matmul(a, lo[:, k, rows], w_hi[:, slot, i], start=False,
                                            stop=(k == KT - 1))
                    if by_row and n == SL_K - 1:
                        last.then_inc(row0_done, 1)
                last.then_inc(w_used[slot], 1)

            def pair_T(rows, bank, tile):
                for i in range(2):
                    for m in range(MT):
                        last = nc.tensor.transpose(bank[:, i * SEQ + m * P:i * SEQ + (m + 1) * P],
                                                   rows[:, m, (tile + i) * P:(tile + i + 1) * P], ident[:])
                return last

            def acc_free(b):
                o = b - 2
                if 0 <= o < 32:
                    pe.wait_ge(rows_out, o + 1)
                if 16 <= o < 20:
                    pe.wait_ge(acc_read, o - 15)
                if o >= 32:
                    pe.wait_ge(y_ready, MT * (o - 31))

            def input_T(layer, h):
                if layer == 0:
                    if h == 0:
                        pe.wait_ge(x0_in, 16)
                    elif h == 1 or h % 2 == 0:
                        pe.wait_ge(x_in[h // 2], 16)
                    if h == 3:
                        pe.wait_ge(vec_ready, 1)
                else:
                    pe.wait_ge(x1_ready, h + 1)
                if h >= 4:
                    pe.wait_ge(xlo_ready, SLICES * layer + h - 3)
                pair_T(xrow, X[h % 4], 2 * h).then_inc(xT_done, 1)

            def staged_products(layer, first, h):
                slot = h % RING
                n = SLICES * layer + h + 1
                passes = [(xT_hi, w_hi, ((xhi_ready, n), (hi_ready[slot], rounds(first, 0, 0, h)))),
                          (xT_lo, w_hi, ((xlo_ready, n),)),
                          (xT_hi, w_lo, ((lo_ready[slot], rounds(first, 0, 0, h)),))]
                if layer:
                    passes[1:] = passes[:0:-1]
                for p, (xs, ws, needs) in enumerate(passes):
                    for which, count in needs:
                        pe.wait_ge(which, count)
                    for i in range(SL_K):
                        k = SL_K * h + i
                        for m in range(MT):
                            last = nc.tensor.matmul(acc[:, first // SLICES % 2, m], xs[:, k, m * P:(m + 1) * P],
                                                    ws[:, slot, i], start=(k == 0 and p == 0), stop=False)
                last.then_inc(w_used[slot], 1)

            def first_block(layer, first, per):
                for h in range(SLICES):
                    if h < STAGED[layer]:
                        staged_products(layer, first, h)
                    else:
                        pe.wait_ge(xlo_ready, SLICES * layer + h + 1)
                        slice_products(first, 0, per, h, xT_hi, xT_lo)
                    if h + 2 < SLICES:
                        input_T(layer, h + 2)

            def keep_clock(n):
                for _ in range(n):
                    nc.tensor.matmul(acc[:, 0, 0], idle[:, 0:P], idle[:], start=True, stop=True)

            pe.wait_ge(const_set, 2)
            keep_clock(6)
            pe.wait_ge(ident_in, 16)
            input_T(0, 0)
            pe.wait_ge(pre_in, 16)
            nc.tensor.transpose(X[3][:, 0:NPRE], pre_rows[:], ident[0:NPRE, 0:NPRE]).then_inc(vec_T, 1)
            keep_clock(5)
            input_T(0, 1)
            first_block(0, S_QKVZ, 32)

            def scores(g, h):
                s = X[h]
                nc.tensor.matmul(s[:, P:2 * P], qT[:, h, P:SEQ], kT[:, h, 0:P], start=True, stop=True)
                diagonal = s[:].rearrange("p (i t k) -> p i t k", i=2, t=2)[:, :, 0]
                nc.tensor.matmul(diagonal, ident_b[:], mask_b[:].rearrange("p (i k) -> p i k", i=1)
                                 .to_broadcast([P, 2, P]), start=True, stop=False)
                nc.tensor.matmul(s[:, 0:P], qT[:, h, 0:P], kT[:, h, 0:P], start=False, stop=False)
                nc.tensor.matmul(s[:, 2 * P:3 * P], qT[:, h, P:SEQ], kT[:, h, P:SEQ], start=False, stop=True
                                 ).then_inc(s_done, 1)

            def probs_T(g, h):
                pe.wait_ge(p_ready, G * g + h + 1)
                for i in range(3):
                    last = nc.tensor.transpose(X[h][:, i * P:(i + 1) * P], probs[:, h, i * P:(i + 1) * P], ident[:])
                last.then_inc(pT_done, 1)

            def values(g):
                pe.wait_ge(pT_ready, G * (g + 1))
                pe.wait_ge(rows_out, 4 * g + 3)
                for h in range(G):
                    c = slice(h * P, (h + 1) * P)
                    nc.tensor.matmul(X[0][:, c], pT[:, h, 0:P], v_row[:, 0, c], start=True, stop=True)
                    nc.tensor.matmul(X[1][:, c], pT[:, h, P:2 * P], v_row[:, 0, c], start=True, stop=False)
                    last = nc.tensor.matmul(X[1][:, c], pT[:, h, 2 * P:3 * P], v_row[:, 1, c],
                                            start=False, stop=True)
                last.then_inc(pv_done, 1)

            def gated_T(g):
                pe.wait_ge(u_ready, g + 1)
                pair_T(u_row, X[2], 0)
                pair_T(u_row, X[3], 2).then_inc(uT_done, 1)

            def group(g, first):
                for s in range(SLICES if first else 0, 4 * SLICES):
                    if s % SLICES == 0 and not (first and s < 2 * SLICES):
                        pe.wait_ge(rows_out, 4 * g + s // SLICES - 1)
                    slice_products(S_QKVZ, g, 32, s, xT_hi, xT_lo)
                    if s == 3 and not first:
                        gated_T(g - 1)
                    if s == 9 and first:
                        pe.wait_ge(vec_in, 16 * 4)
                        nc.tensor.transpose(X[1][:, 0:NVEC], vec_rows[:], ident[0:NVEC, 0:NVEC])
                        pe.wait_ge(dw_in, 16)
                        for q in range(4):
                            last = nc.tensor.transpose(X[0][:, q * DW_ROWS:(q + 1) * DW_ROWS], dw_rows[:, q, :],
                                                       ident[0:DW_ROWS, 0:DW_ROWS])
                        last.then_inc(vec_T, 1)
                    if s == 14:
                        pe.wait_ge(rope_step, 6 * g + 3)
                        if first:
                            pe.wait_ge(vec_ready, 2)
                        else:
                            pe.wait_ge(u_ready, g)
                        pair_T(q_row, X[0], 0)
                        pair_T(q_row, X[1], 2).then_inc(qT_done, 1)
                    if s == 20:
                        pe.wait_ge(rope_step, 6 * g + 6)
                        if not first:
                            pe.wait_ge(ulo_ready, g)
                        pair_T(k_row, X[2], 0)
                        pair_T(k_row, X[3], 2).then_inc(kT_done, 1)
                    if s == 22:
                        if first:
                            pe.wait_ge(mask_ready, 2)
                        pe.wait_ge(qT_ready, g + 1)
                        pe.wait_ge(kT_ready, g + 1)
                        for h in range(G):
                            scores(g, h)
                    if s in (26, 27):
                        for h in (0, 1) if s == 26 else (2, 3):
                            probs_T(g, h)
                    if s == 30:
                        values(g)

            group(0, True)
            with pe.Fori(1, NG) as g:
                group(g, False)

            for s in range(4 * SLICES):
                if s % SLICES == 0:
                    acc_free(16 + s // SLICES)
                if s % 2 == 0 and s < SLICES:
                    pe.wait_ge(ulo_ready, s // 2 + 1)
                slice_products(S_OUT0, 0, 0, s, uT_hi, uT_lo, by_row=(s == 4 * SLICES - 1))
                if s == 3:
                    gated_T(NG - 1)

            acc_free(20)
            pe.wait_ge(ulo_ready, NG)
            keep_clock(11)
            input_T(1, 0)
            keep_clock(1)
            input_T(1, 1)
            first_block(1, S_AG, 16)

            def conv_input_pair(h, buf, first):
                pe.wait_ge(rows_out, 20 + h + 1)
                if not first:
                    pe.wait_ge(sig_ready, h)
                pair_T(ag_row[:, buf], X[0], 0)
                pair_T(ag_row[:, buf], X[1], 2).then_inc(agT_done, 1)

            def two_blocks(i, first):
                for s in range(SLICES if first else 0, 2 * SLICES):
                    if s % SLICES == 0:
                        if first:
                            acc_free(20 + s // SLICES)
                        else:
                            pe.wait_ge(rows_out, 20 + 2 * i + s // SLICES - 1)
                    slice_products(S_AG, i, 16, s, xT_hi, xT_lo)
                    if s == 1 and not first:
                        conv_input_pair(2 * i - 1, 1, False)
                    if s == 9:
                        conv_input_pair(2 * i, 0, first)

            two_blocks(0, True)
            with pe.Fori(1, NG) as i:
                two_blocks(i, False)

            def conv_rows(j):
                pe.wait_ge(conv_done, G * (j + 1))
                if j:
                    pe.wait_ge(c_ready, MT * j)
                else:
                    pe.wait_ge(sig_ready, 2 * NG)
                for m in range(MT):
                    for c in range(G):
                        last = nc.tensor.transpose(X[3 - 3 * m][:, c * P:(c + 1) * P],
                                                   cT[:, G * j + c, m * P:(m + 1) * P], ident[:])
                    last.then_inc(cR_done, 1)

            def final_T(n):
                pe.wait_ge(norm_ready, n + 1)
                pe.wait_ge(rows_out, 28 + n + 1)
                if n:
                    pe.wait_ge(silu_ready, n)
                    pe.wait_ge(t_ready, n)
                for b in range(2):
                    pair_T(c_row, X[b], 4 * n + 2 * b)
                    last = pair_T(z_row1, X[2 + b], 4 * n + 2 * b)
                last.then_inc(fT_done, 1)

            for s in range(4 * SLICES):
                if s % SLICES == 0:
                    acc_free(28 + s // SLICES)
                slice_products(S_Z, 0, 0, s, xT_hi, xT_lo)
                if s == 1:
                    conv_input_pair(2 * NG - 1, 1, False)
                if s in ROWS_AT:
                    conv_rows(ROWS_AT.index(s))
                if s in FINAL_AT:
                    final_T(FINAL_AT.index(s))

            for s in range(4 * SLICES):
                if s % SLICES == 0:
                    acc_free(32 + s // SLICES)
                if s < SLICES and s % 2 == 0:
                    pe.wait_ge(vlo_ready, s // 2 + 1)
                slice_products(S_OUT1, 0, 0, s, vT_hi, vT_lo, by_row=(s == 4 * SLICES - 1))
                if s in (0, 2):
                    final_T(2 + s // 2)

        @block.scalar
        def _(act):
            def high(first, it, per, s):
                u = first // 2 + s // 2
                slot = s % RING
                if isinstance(it, int) and first + it == 0 and s in (0, 2):
                    act.wait_ge(half_in[s // 2], 16)
                else:
                    act.wait_ge(raw_ready[u % LOADS], loaded(first, it, per, s))
                if first or not isinstance(it, int) or it or s >= RING:
                    act.wait_ge(w_used[slot], rounds(first - RING, it, per, s))
                half = s % 2
                nc.scalar.activation(w_hi[:, slot], raw[:, u % LOADS, 2 * half:2 * half + 2], ACT.Copy
                                     ).then_inc(hi_ready[slot], 1)

            def block_rows(first, it, per, s, dst, scale, func=ACT.Copy):
                act.wait_ge(w_used[RING - 1], rounds(first, it, per, s))
                par = ((first + s) // SLICES) % 2
                for m in range(MT):
                    last = nc.scalar.activation(dst[:, m], acc[:, par, m], func, scale=scale[:, m:m + 1])
                last.then_inc(rows_out, 1)

            def input_high(layer, n, vcol):
                act.wait_ge(xT_done, SLICES * layer + n + 1)
                for c in range(2):
                    t = 2 * n + c
                    last = nc.scalar.activation(
                        xT_hi[:, t], X[n % 4][:, c * SEQ:(c + 1) * SEQ], ACT.Copy,
                        scale=vec[:, vcol + t:vcol + t + 1])
                last.then_inc(xhi_ready, 1)

            def squares(junk, row, m, n, before):
                if before:
                    act.wait_ge(ssq_ready, before)
                nc.scalar.activation(junk, row, ACT.Square, accum_out=ssq[:, m, n:n + 1]).then_inc(ssq_ready, 1)

            act.dma_start(pre_rows[:], pre_g.rearrange("l (t c) -> (l t) c", c=P)).then_inc(pre_in, 16)

            act.wait_ge(vec_T, 1)
            nc.scalar.activation(vec[:, 0:NPRE], X[3][:, 0:NPRE], ACT.Copy).then_inc(vec_ready, 1)
            act.wait_ge(vec_ready, 1)
            def input_squares(junk, n, m, before):
                squares(junk, xrow[:, m, n * NCOL:(n + 1) * NCOL], m, n, before)

            act.wait_ge(x0_in, 16)
            for h in range(SLICES):
                input_high(0, h, V_PRE0)
                for s in SPLIT_AFTER[h]:
                    high(S_QKVZ, 0, 32, s)
                if h in SQUARES_AFTER:
                    n = SQUARES_AFTER.index(h)
                    act.wait_ge(x_in[n // 2], 16)
                    input_squares(junk0[:], n // 2, n % 2, n)
            for n in range(len(SQUARES_AFTER), SLICES):
                act.wait_ge(x_in[n // 2], 16)
                input_squares(junk0[:], n // 2, n % 2, n)

            def heads_high(g):
                act.wait_ge(uT_done, g + 1)
                for b in range(2):
                    last = nc.scalar.activation(uT_hi[:, bass.ds(g * 4 + 2 * b, 2)], X[2 + b][:], ACT.Copy)
                last.then_inc(uhi_ready, 1)

            def group_end(s, g):
                if s == 3:
                    if not (isinstance(g, int) and g == 0):
                        act.wait_ge(u_ready, g)
                    block_rows(S_QKVZ, g, 32, 31, z_row, rms[0], ACT.Silu)
                if s == 7:
                    heads_high(g)

            def exponentials(g, h, first):
                if h == 0 and not first:
                    act.wait_ge(pT_done, G * g)
                act.wait_ge(negmax_ready, G * g + h + 1)
                for m in range(MT):
                    c = slice(0, P) if m == 0 else slice(P, 3 * P)
                    last = nc.scalar.activation(probs[:, h, c], X[h][:, c], ACT.Exp, bias=neg_max[:, h, m:m + 1],
                                                scale=SCALE, accum_out=row_sum[:, h, m:m + 1])
                last.then_inc(p_ready, 1)

            def group(g, first):
                for s in range(SLICES + LEAD if first else 0, 4 * SLICES):
                    high(S_QKVZ, g, 32, s)
                    if not first:
                        group_end(s, g - 1)
                    if s == 12 and first:
                        act.wait_ge(vec_T, 2)
                        nc.scalar.activation(vec[:, NPRE:NPRE + NVEC], X[1][:, 0:NVEC], ACT.Copy)
                        nc.scalar.activation(taps[:], X[0][:, 0:TAPS * KT], ACT.Copy).then_inc(vec_ready, 1)
                    if s == 11:
                        if first:
                            act.wait_ge(rms_ready, 1)
                        block_rows(S_QKVZ, g, 32, 7, q_row, rms[0])
                    if s == 18:
                        act.wait_ge(qT_done, g + 1)
                        for b in range(2):
                            last = nc.scalar.activation(qT[:, 2 * b:2 * b + 2], X[b][:], ACT.Copy)
                        last.then_inc(qT_ready, 1)
                    if s == 19:
                        block_rows(S_QKVZ, g, 32, 15, k_row, rms[0])
                    if s == 24:
                        act.wait_ge(kT_done, g + 1)
                        for b in range(2):
                            last = nc.scalar.activation(kT[:, 2 * b:2 * b + 2], X[2 + b][:], ACT.Copy)
                        last.then_inc(kT_ready, 1)
                    if s == 27:
                        if not first:
                            act.wait_ge(pv_done, g)
                        block_rows(S_QKVZ, g, 32, 23, v_row, rms[0])
                    if s in (26, 27, 28, 29):
                        exponentials(g, s - 26, first)

            group(0, True)
            with act.Fori(1, NG) as g:
                group(g, False)

            def out0_squares(n):
                for m in range(MT):
                    if n == NG - 1 and m == 0:
                        act.wait_ge(row0_done, 1)
                    else:
                        act.wait_ge(w_used[RING - 1], rounds(S_OUT0, 0, 0, 8 * n + 7))
                    squares(junk1[:], acc[:, n % 2, m], m, n, 8 + MT * n + m)
                act.wait_ge(ssq_ready, 8 + MT * (n + 1))
                act.sem_inc(rows_out, 1)

            for s in range(4 * SLICES):
                high(S_OUT0, 0, 0, s)
                group_end(s, NG - 1)
                if s % SLICES == 3 and s > SLICES:
                    out0_squares(s // SLICES - 1)
            for s in range(RING - 1):
                high(S_AG, 0, 16, s)
            out0_squares(NG - 1)
            high(S_AG, 0, 16, RING - 1)
            for h in range(SLICES):
                input_high(1, h, V_PRE1)
                if h + LEAD >= RING:
                    high(S_AG, 0, 16, h + LEAD)
                if h:
                    act.wait_ge(x1_ready, h + 1)
                    input_squares(junk2[:], (h - 1) // 2, (h - 1) % 2, 16 + h - 1)
            input_squares(junk2[:], NG - 1, 1, 16 + SLICES - 1)

            def conv_input_parts(h, buf, first):
                act.wait_ge(agT_done, h + 1)
                if not first:
                    act.wait_ge(gated, h - 1)
                for c in range(2):
                    last = nc.scalar.activation(u_pad[:, bass.ds(h * 2 + c, 1), PAD:UW],
                                                X[0][:, c * SEQ:(c + 1) * SEQ], ACT.Identity,
                                                bias=vec[:, bass.ds(h * 2 + V_BA + c, 1)])
                for c in range(2):
                    last = nc.scalar.activation(sig[:, buf, c], X[1][:, c * SEQ:(c + 1) * SEQ], ACT.Sigmoid,
                                                bias=vec[:, bass.ds(h * 2 + V_BG + c, 1)])
                last.then_inc(sig_ready, 1)

            def two_blocks(i, first):
                for s in range(SLICES + LEAD if first else 0, 2 * SLICES):
                    high(S_AG, i, 16, s)
                    if s == 3 and not first:
                        block_rows(S_AG, i - 1, 16, 15, ag_row[:, 1], rms[2])
                    if s == 5 and not first:
                        conv_input_parts(2 * i - 1, 1, False)
                    if s == 11:
                        if first:
                            act.wait_ge(rms_ready, 3)
                        block_rows(S_AG, i, 16, 7, ag_row[:, 0], rms[2])
                    if s == 13:
                        if first:
                            act.wait_ge(pad_set, 1)
                        conv_input_parts(2 * i, 0, first)

            two_blocks(0, True)
            with act.Fori(1, NG) as i:
                two_blocks(i, False)

            for s in range(4 * SLICES):
                high(S_Z, 0, 0, s)
                if s == 3:
                    block_rows(S_AG, NG - 1, 16, 15, ag_row[:, 1], rms[2])
                if s == 5:
                    conv_input_parts(2 * NG - 1, 1, False)
                if s % SLICES == 3 and s > SLICES:
                    n = s // SLICES - 1
                    block_rows(S_Z, 0, 0, 8 * n + 7, z_row1[:, :, n * NCOL:(n + 1) * NCOL], rms[2], ACT.Silu)
                for j in range(NG):
                    for m in range(MT):
                        if s == ROWS_AT[j] + 3:
                            act.wait_ge(cR_done, MT * j + m + 1)
                            nc.scalar.activation(c_row[:, m, j * NCOL:(j + 1) * NCOL], X[3 - 3 * m][:], ACT.Copy
                                                 ).then_inc(c_ready, 1)

            def affine_silu(n):
                act.wait_ge(fT_done, n + 1)
                if n:
                    act.wait_ge(vlo_ready, n)
                for c in range(4):
                    t = 4 * n + c
                    last = nc.scalar.activation(t_buf[:, c], X[c // 2][:, (c % 2) * SEQ:(c % 2 + 1) * SEQ], ACT.Silu,
                                                scale=vec[:, V_LNG + t:V_LNG + t + 1],
                                                bias=vec[:, V_LNB + t:V_LNB + t + 1])
                last.then_inc(silu_ready, 1)

            def final_high(n):
                act.wait_ge(t_ready, n + 1)
                nc.scalar.activation(vT_hi[:, 4 * n:4 * n + 4], t_buf[:], ACT.Copy).then_inc(vhi_ready, 1)

            def out1_squares(n):
                for m in range(MT):
                    act.wait_ge(y_ready, MT * n + m + 1)
                    squares(junk1[:], y1[:, m, n * NCOL:(n + 1) * NCOL], m, n, 24 + MT * n + m)

            for s in range(4 * SLICES):
                high(S_OUT1, 0, 0, s)
                if s in (0, 2, 4, 6):
                    affine_silu(s // 2)
                if s in (1, 3, 5, 7):
                    final_high(s // 2)
                if s == 3:
                    block_rows(S_Z, 0, 0, 31, z_row1[:, :, 3 * NCOL:4 * NCOL], rms[2], ACT.Silu)
                if s % SLICES == 4 and s > SLICES:
                    out1_squares(s // SLICES - 1)
            out1_squares(NG - 1)
            act.wait_ge(yg_ready, MT * NG)
            act.wait_ge(rms_ready, 4)
            for m in range(MT):
                part = yg1[:, m, POOL_COLS]
                nc.scalar.activation(part, part, ACT.Copy, scale=rms[3][:, m:m + 1]).then_inc(scaled, 1)

        @block.vector
        def _(dve):
            def low(first, it, per, s):
                u = first // 2 + s // 2
                slot = s % RING
                half = s % 2
                dve.wait_ge(hi_ready[slot], rounds(first, it, per, s))
                nc.vector.tensor_tensor(w_lo[:, slot], raw[:, u % LOADS, 2 * half:2 * half + 2], rd(w_hi, slot),
                                        ALU.subtract).then_inc(lo_ready[slot], 1)

            def input_low(layer, n, vcol):
                dve.wait_ge(xhi_ready, SLICES * layer + n + 1)
                for c in range(2):
                    t = 2 * n + c
                    last = nc.vector.scalar_tensor_tensor(
                        out=xT_lo[:, t], in0=X[n % 4][:, c * SEQ:(c + 1) * SEQ],
                        scalar=vec[:, vcol + t:vcol + t + 1], in1=xT_hi[:, t].bitcast(f32),
                        op0=ALU.mult, op1=ALU.subtract)
                last.then_inc(xlo_ready, 1)

            def mean_square(first):
                nc.vector.tensor_scalar(mean_sq, first, 1.0 / D, RMS_EPS, ALU.mult, ALU.add).then_inc(ms_ready, 1)

            def mean_of_parts(ready, count):
                dve.wait_ge(ssq_ready, ready)
                nc.vector.reduce_sum(mean_sum, ssq, AX.X).then_inc(sum_ready, 1)
                dve.wait_ge(sum_ready, count)
                mean_square(mean_sum)

            for h in range(SLICES):
                input_low(0, h, V_PRE0)
                for s in SPLIT_AFTER[h]:
                    low(S_QKVZ, 0, 32, s)
            dve.wait_ge(rope_in, 48)
            dve.wait_ge(ident_in, 16)
            nc.vector.tensor_copy(ident_b[:], ident[:]).then_inc(mask_ready, 1)
            nc.vector.tensor_copy(mask_b[:], mask[:]).then_inc(mask_ready, 1)
            mean_of_parts(8, 1)

            def gate_outputs(g):
                dve.wait_ge(pv_done, g + 1)
                dve.wait_ge(rows_out, 4 * (g + 1))
                dve.wait_ge(inv_ready, g + 1)
                for m in range(MT):
                    for h in range(G):
                        c = slice(h * P, (h + 1) * P)
                        last = nc.vector.scalar_tensor_tensor(
                            out=u_row[:, m, c], in0=X[m][:, c], scalar=inv_sum[:, h, m:m + 1], in1=z_row[:, m, c],
                            op0=ALU.mult, op1=ALU.mult)
                last.then_inc(u_ready, 1)

            def heads_low(g):
                dve.wait_ge(uhi_ready, g + 1)
                for b in range(2):
                    t = bass.ds(g * 4 + 2 * b, 2)
                    last = nc.vector.tensor_tensor(uT_lo[:, t], X[2 + b][:].rearrange("p (t r) -> p t r", t=2),
                                                   uT_hi[:, t].bitcast(f32), ALU.subtract)
                last.then_inc(ulo_ready, 1)

            def group_end(s, g):
                if s == 4:
                    gate_outputs(g)
                if s == 7:
                    heads_low(g)

            def maxima(g, h):
                dve.wait_ge(s_done, G * g + h + 1)
                nc.vector.reduce_max(row_max[:, h, 0:1], X[h][:, 0:P], AX.X)
                nc.vector.reduce_max(row_max[:, h, 1:2], X[h][:, P:3 * P], AX.X).then_inc(max_ready, 1)
                dve.wait_ge(max_ready, G * g + h + 1)
                nc.vector.tensor_scalar(neg_max[:, h], row_max[:, h], -SCALE, None, ALU.mult
                                        ).then_inc(negmax_ready, 1)

            def group(g, first):
                for s in range(SLICES + LEAD if first else 0, 4 * SLICES):
                    low(S_QKVZ, g, 32, s)
                    if not first:
                        group_end(s, g - 1)
                    if s in (26, 27):
                        for h in (0, 1) if s == 26 else (2, 3):
                            maxima(g, h)
                    if s in (30, 31):
                        for h in (0, 1) if s == 30 else (2, 3):
                            dve.wait_ge(pT_done, G * g + h + 1)
                            nc.vector.tensor_copy(pT[:, h], X[h][:, 0:3 * P]).then_inc(pT_ready, 1)
                    if s == 31:
                        dve.wait_ge(p_ready, G * g + 4)
                        nc.vector.reciprocal(small[:, 44:52], small[:, 36:44]).then_inc(inv_ready, 1)

            group(0, True)
            with dve.Fori(1, NG) as g:
                group(g, False)

            def out0_rows(n, ms=(0, 1)):
                if n == 0:
                    dve.wait_ge(gpost0_in, 16)
                for m in ms:
                    dve.wait_ge(ssq_ready, 8 + MT * n + m + 1)
                    c = slice(n * NCOL, (n + 1) * NCOL)
                    last = nc.vector.tensor_tensor(y0[:, m, c], acc[:, n % 2, m], gpost0[:, c], ALU.mult)
                    if m == 1:
                        last.then_inc(acc_read, 1)

            for s in range(4 * SLICES):
                low(S_OUT0, 0, 0, s)
                group_end(s, NG - 1)
                if s % SLICES == 3 and s > SLICES:
                    out0_rows(s // SLICES - 1)
            def mean_but_last(ready, count):
                dve.wait_ge(ssq_ready, ready)
                nc.vector.reduce_sum(mean_sum, ssq[:, :, 0:NG - 1], AX.X).then_inc(sum_ready, 1)
                dve.wait_ge(sum_ready, count)
                nc.vector.tensor_scalar(mean_part, mean_sum, 1.0 / D, RMS_EPS, ALU.mult, ALU.add
                                        ).then_inc(part_ready, 1)

            def mean_with_last(ready, part):
                dve.wait_ge(ssq_ready, ready)
                dve.wait_ge(part_ready, part)
                nc.vector.scalar_tensor_tensor(out=mean_sq, in0=ssq[:, :, NG - 1], scalar=1.0 / D, in1=mean_part,
                                               op0=ALU.mult, op1=ALU.add).then_inc(ms_ready, 1)

            mean_but_last(14, 2)
            out0_rows(NG - 1, (0,))

            def residual(c, r, y, done):
                for m in range(MT):
                    last = nc.vector.scalar_tensor_tensor(
                        out=xrow[:, m, c], in0=y[:, m, c], scalar=rms[r][:, m:m + 1], in1=xrow[:, m, c],
                        op0=ALU.mult, op1=ALU.add)
                last.then_inc(done, 1)

            mean_with_last(16, 1)
            out0_rows(NG - 1, (1,))
            dve.wait_ge(rms_ready, 2)
            dve.wait_ge(acc_read, NG)
            residual(slice(0, SEQ), 1, y0, x1_ready)
            for h in range(SLICES):
                if h + 1 < SLICES:
                    residual(slice((h + 1) * SEQ, (h + 2) * SEQ), 1, y0, x1_ready)
                input_low(1, h, V_PRE1)
            dve.wait_ge(x1_ready, SLICES)
            nc.vector.memset(u_pad[:, :, 0:PAD], 0.0).then_inc(pad_set, 1)
            mean_of_parts(24, 3)
            dve.wait_ge(pad_set, 1)

            def conv_tap(tile, c, k, steps):
                part = X[2][:, c * SEQ:(c + 1) * SEQ]
                last = k == TAPS - 1
                u = u_pad[:, bass.ds(tile, 1), k:k + SEQ]
                out_ = cT[:, bass.ds(tile, 1)] if last else part
                if k == 0:
                    ins = nc.vector.tensor_scalar(part, u, taps[:, bass.ds(tile, 1)],
                                                  vec[:, bass.ds(tile + V_BDW, 1)], ALU.mult, ALU.add)
                else:
                    dve.wait_ge(conv_step, steps)
                    ins = nc.vector.scalar_tensor_tensor(
                        out=out_, in0=u, scalar=taps[:, bass.ds(tile + k * KT, 1)], in1=part,
                        op0=ALU.mult, op1=ALU.add)
                ins.then_inc(conv_done if last else conv_step, 1)

            per_pair = 2 * (TAPS - 1)
            with dve.Fori(0, SLICES) as h:
                dve.wait_ge(sig_ready, h + 1)
                pair = u_pad[:, bass.ds(h * 2, 2), PAD:UW]
                nc.vector.tensor_tensor(pair, pair, sig[:, bass.ds(h % 2, 1)].rearrange(
                    "p b c r -> p (b c) r"), ALU.mult).then_inc(gated, 1)
                dve.wait_ge(gated, h + 1)
                for k in range(TAPS):
                    for c in range(2):
                        conv_tap(h * 2 + c, c, k, h * per_pair + 2 * k - 1 + c)

            for n in range(NG):
                for m in range(MT):
                    dve.wait_ge(c_ready, MT * n + m + 1)
                    nc.vector.bn_stats(bn[:, m, n], c_row[:, m, n * NCOL:(n + 1) * NCOL]).then_inc(bn_ready, 1)
            dve.wait_ge(bn_ready, MT * NG)
            for m in range(MT):
                nc.vector.bn_aggr(mv[:, m], bn[:, m]).then_inc(mv_ready, 1)
            dve.wait_ge(mv_ready, MT)
            nc.vector.tensor_scalar(var_eps, mv[:, :, 1], LN_EPS, None, ALU.add).then_inc(var_ready, 1)
            dve.wait_ge(rstd_ready, 1)
            for n in range(NG):
                for m in range(MT):
                    c = c_row[:, m, n * NCOL:(n + 1) * NCOL]
                    last = nc.vector.tensor_scalar(c, c, mv[:, m, 0:1], rstd[:, m:m + 1], ALU.subtract, ALU.mult)
                last.then_inc(norm_ready, 1)

            for n in range(NG):
                dve.wait_ge(silu_ready, n + 1)
                for b in range(2):
                    part = t_buf[:, 2 * b:2 * b + 2]
                    last = nc.vector.tensor_tensor(part, part, X[2 + b][:].rearrange("p (t r) -> p t r", t=2), ALU.mult)
                last.then_inc(t_ready, 1)
                dve.wait_ge(vhi_ready, n + 1)
                nc.vector.tensor_tensor(vT_lo[:, 4 * n:4 * n + 4], t_buf[:], vT_hi[:, 4 * n:4 * n + 4].bitcast(f32),
                                        ALU.subtract).then_inc(vlo_ready, 1)

            def out1_biased(n, m):
                if n == NG - 1 and m == 0:
                    dve.wait_ge(row0_done, 2)
                else:
                    dve.wait_ge(w_used[RING - 1], rounds(S_OUT1, 0, 0, 8 * n + 7))
                if n == 0:
                    dve.wait_ge(bcast1_in, 32)
                c = slice(n * NCOL, (n + 1) * NCOL)
                nc.vector.tensor_tensor(y1[:, m, c], acc[:, n % 2, m], bout[:, c], ALU.add).then_inc(y_ready, 1)

            def out1_gained(n, m):
                dve.wait_ge(y_ready, MT * n + m + 1)
                c = slice(n * NCOL, (n + 1) * NCOL)
                nc.vector.tensor_tensor(yg1[:, m, c], y1[:, m, c], gpost1[:, c], ALU.mult).then_inc(yg_ready, 1)

            for s in range(SLICES, 4 * SLICES):
                low(S_OUT1, 0, 0, s)
                if s % SLICES == 3:
                    for m in range(MT):
                        out1_biased(s // SLICES - 1, m)
                    for m in range(MT):
                        out1_gained(s // SLICES - 1, m)
            mean_but_last(30, 4)
            out1_biased(NG - 1, 0)
            out1_gained(NG - 1, 0)
            out1_biased(NG - 1, 1)
            mean_with_last(32, 2)
            out1_gained(NG - 1, 1)
            dve.wait_ge(rms_ready, 4)
            dve.wait_ge(yg_ready, MT * NG)
            for c in OUT_PARTS:
                residual(c, 3, yg1, o_ready)

        @block.gpsimd
        def _(pool):
            nc.gpsimd.memset(idle[:], 0.0).then_inc(const_set, 1)
            nc.gpsimd.memset(m_half, -0.5).then_inc(const_set, 1)
            pool.wait_ge(const_set, 2)

            def inverse_root(out_, in_, ready, count, done):
                pool.wait_ge(ready, count)
                nc.gpsimd.tensor_tensor(out_, in_, m_half, ALU.pow).then_inc(done, 1)

            inverse_root(rms[0], mean_sq, ms_ready, 1, rms_ready)
            pool.wait_ge(rope_in, 48)

            def rotate(row, block_no, steps):
                pool.wait_ge(rows_out, block_no)
                for m in range(MT):
                    v = row[:, m].rearrange("p (h d) -> p h d", h=G)
                    t = rope_t[:, m].rearrange("p (h d) -> p h d", h=G)
                    for a in range(2):
                        o = slice(a * HALF, (a + 1) * HALF)
                        w = slice((1 - a) * HALF, (2 - a) * HALF)
                        last = nc.gpsimd.tensor_tensor(
                            t[:, :, o], v[:, :, w], sin_t[:, m:m + 1, o].to_broadcast([P, G, HALF]), ALU.mult)
                last.then_inc(rope_step, 1)
                pool.wait_ge(rope_step, steps + 1)
                for m in range(MT):
                    v = row[:, m].rearrange("p (h d) -> p h d", h=G)
                    last = nc.gpsimd.tensor_tensor(v, v, cos_t[:, m:m + 1, :].to_broadcast([P, G, P]), ALU.mult)
                last.then_inc(rope_step, 1)
                pool.wait_ge(rope_step, steps + 2)
                last = nc.gpsimd.tensor_tensor(row[:], row[:], rope_t[:], ALU.add)
                last.then_inc(rope_step, 1)

            with pool.Fori(0, NG) as g:
                rotate(q_row, 4 * g + 1, 6 * g)
                rotate(k_row, 4 * g + 2, 6 * g + 3)

            def low(first, it, per, s):
                u = first // 2 + s // 2
                slot = s % RING
                half = s % 2
                pool.wait_ge(hi_ready[slot], rounds(first, it, per, s))
                nc.gpsimd.tensor_tensor(w_lo[:, slot], raw[:, u % LOADS, 2 * half:2 * half + 2], rd(w_hi, slot),
                                        ALU.subtract).then_inc(lo_ready[slot], 1)

            for s in range(RING - 1):
                low(S_AG, 0, 16, s)
            inverse_root(rms[1], mean_sq, ms_ready, 2, rms_ready)
            for s in range(RING - 1, 10):
                low(S_AG, 0, 16, s)
            inverse_root(rms[2], mean_sq, ms_ready, 3, rms_ready)
            for s in range(10, 2 * SLICES):
                low(S_AG, 0, 16, s)
            with pool.Fori(1, NG) as j:
                for s in range(2 * SLICES):
                    low(S_AG, j, 16, s)
            for s in range(4 * SLICES):
                if s == ROOT_AT:
                    inverse_root(rstd, var_eps, var_ready, 1, rstd_ready)
                low(S_Z, 0, 0, s)
            for s in range(SLICES):
                low(S_OUT1, 0, 0, s)
            inverse_root(rms[3], mean_sq, ms_ready, 4, rms_ready)
            for m in range(MT):
                pool.wait_ge(scaled, m + 1)
                c = xrow[:, m, POOL_COLS]
                nc.gpsimd.tensor_tensor(c, c, yg1[:, m, POOL_COLS], ALU.add).then_inc(o_pool, 1)


_ROPE_THETA = 10000.0


def kernel(x, pre_norm_g, post_norm_g, attn_w_in, attn_w_out, conv_w_in, conv_b_in, conv_w_dw, conv_b_dw,
           conv_ln_g, conv_ln_b, conv_w_out, conv_b_out):
    import concourse.bacc as bacc
    from concourse.bass_utils import run_bass_kernel_spmd

    inv_freq = (1.0 / (_ROPE_THETA ** (np.arange(HALF, dtype=np.float32) * 2.0 / P))).astype(np.float32)
    ang = np.arange(SEQ, dtype=np.float32)[:, None] * inv_freq[None, :]
    cos, sin = np.cos(ang), np.sin(ang)
    by_row = lambda a: np.ascontiguousarray(a.reshape(MT, P, P).transpose(1, 0, 2), np.float32)
    ins = dict(
        x=x, pre_g=pre_norm_g, post_g=post_norm_g, w_in0=attn_w_in, w_out0=attn_w_out, w_in1=conv_w_in,
        b_in=conv_b_in, w_dw=conv_w_dw, b_dw=conv_b_dw, ln_g=conv_ln_g, ln_b=conv_ln_b, w_out1=conv_w_out,
        b_out=conv_b_out,
        rope_cos=by_row(np.concatenate([cos, cos], 1)), rope_sin=by_row(np.concatenate([-sin, sin], 1)),
        identity=np.eye(P, dtype=np.float32), causal=np.triu(np.full((P, P), -1e30, np.float32), 1))

    nc = bacc.Bacc("TRN2", target_bir_lowering=False, num_devices=1)
    arrays, args = {}, {}
    for name, value in ins.items():
        a = np.ascontiguousarray(value)
        arrays[f"in_{name}"] = a
        args[name] = nc.dram_tensor(f"in_{name}", a.shape, mybir.dt.from_np(a.dtype), kind="ExternalInput").ap()
    args["out"] = nc.dram_tensor("out", (1, SEQ, D), mybir.dt.float32, kind="ExternalOutput").ap()
    build(nc, **args)
    r = run_bass_kernel_spmd(nc, [arrays], core_ids=[0])
    return r.results[0]["out"]
```
